# Optimizing a Trainium2 kernel written in Bass

```python
import math
import jax, jax.numpy as jnp
from jax import lax
import numpy as np

D_MODEL = 2048
BATCH = 1
SEQ = 512
DEPTH = 1

DN_H = 8
DN_DK = 128
DN_DV = 128
DN_CHUNK = 64
CONV_K = 5
SWA_HQ = 8
SWA_HKV = 2
SWA_HD = 128
WINDOW = 128
BLOCK = 128
ROPE_DIM = SWA_HD // 4
ROPE_THETA = 500000.0
D_FF = 4 * D_MODEL
EPS = 1e-6

DN_QK = DN_H * DN_DK
DN_V = DN_H * DN_DV
DN_CONV_CH = 2 * DN_QK + DN_V
IN_SIZES = (DN_CONV_CH, DN_V, 2 * DN_H, 2 * DN_H, SWA_HQ * SWA_HD, 2 * SWA_HKV * SWA_HD, 2 * D_MODEL)
IN_WIDTH = DN_CONV_CH + DN_V + 4 * DN_H + SWA_HQ * SWA_HD + 2 * SWA_HKV * SWA_HD + 2 * D_MODEL

kernel_name = "hybrid_deltanet_swa_adaln_block"

def split_last(t, sizes):
    idx = np.cumsum(np.array(sizes))[:-1].tolist()
    return jnp.split(t, idx, axis=-1)

def rms_norm(x, w):
    xf = x.astype(jnp.float32)
    y = xf * lax.rsqrt(jnp.mean(jnp.square(xf), axis=-1, keepdims=True) + EPS)
    return (y * w.astype(jnp.float32)).astype(x.dtype)

def l2_normalize(x):
    xf = x.astype(jnp.float32)
    return xf * lax.rsqrt(jnp.sum(jnp.square(xf), axis=-1, keepdims=True) + EPS)

def centred_depthwise_conv(x, w):
    k_size, ch = w.shape
    pad = (k_size - 1) // 2
    return lax.conv_general_dilated(x, w[:, None, :], window_strides=(1,), padding=((pad, pad),),
                                    dimension_numbers=('NWC', 'WIO', 'NWC'), feature_group_count=ch)

def gated_delta_chunked(q, k, v, g, beta):
    B, L, H, DK = q.shape
    DV = v.shape[-1]
    C = DN_CHUNK
    N = L // C
    f32 = jnp.float32

    def chunks(t):
        return t.astype(f32).reshape(B, N, C, H, -1).transpose(0, 3, 1, 2, 4)

    q, k, v = chunks(q), chunks(k), chunks(v)
    g = jnp.cumsum(chunks(g[..., None])[..., 0], axis=-1)
    beta = chunks(beta[..., None])[..., 0]
    k_beta = k * beta[..., None]
    v_beta = v * beta[..., None]
    incl = jnp.tril(jnp.ones((C, C), dtype=bool))
    strict = jnp.tril(jnp.ones((C, C), dtype=bool), -1)
    decay = jnp.exp(jnp.where(incl, g[..., :, None] - g[..., None, :], -jnp.inf))
    a_kk = jnp.where(strict, jnp.einsum('bhncd,bhnsd->bhncs', k_beta, k) * decay, 0.0)
    eye = jnp.eye(C, dtype=f32)
    t_inv = lax.linalg.triangular_solve(eye + a_kk, jnp.broadcast_to(eye, a_kk.shape),
                                        left_side=True, lower=True, unit_diagonal=True)
    u = jnp.einsum('bhncs,bhnse->bhnce', t_inv, v_beta)
    w = jnp.einsum('bhncs,bhnsd->bhncd', t_inv, k_beta * jnp.exp(g)[..., None])
    a_qk = jnp.einsum('bhncd,bhnsd->bhncs', q, k) * decay
    g_last = g[..., -1]
    q_dec = q * jnp.exp(g)[..., None]
    k_dec = k * jnp.exp(g_last[..., None] - g)[..., None]

    def step(state, inp):
        q_i, w_i, u_i, a_i, k_i, gl_i = inp
        v_new = u_i - jnp.einsum('bhcd,bhde->bhce', w_i, state)
        o_i = jnp.einsum('bhcd,bhde->bhce', q_i, state) + jnp.einsum('bhcs,bhse->bhce', a_i, v_new)
        state = state * jnp.exp(gl_i)[..., None, None] + jnp.einsum('bhcd,bhce->bhde', k_i, v_new)
        return state, o_i

    xs = tuple(jnp.moveaxis(t, 2, 0) for t in (q_dec, w, u, a_qk, k_dec, g_last))
    s0 = jnp.zeros((B, H, DK, DV), f32)
    _, o = lax.scan(step, s0, xs)
    return o.transpose(1, 0, 3, 2, 4).reshape(B, L, H, DV)

def reverse_seq(t):
    return jnp.flip(t, axis=1)

def deltanet_branch(qkv, z, beta_logits, a, conv_w, a_log, dt_bias, out_norm_w):
    B, L, _ = qkv.shape
    f32 = jnp.float32
    qkv = jax.nn.silu(centred_depthwise_conv(qkv, conv_w))
    q, k, v = split_last(qkv, (DN_QK, DN_QK, DN_V))
    q = l2_normalize(q.reshape(B, L, DN_H, DN_DK)) * (DN_DK ** -0.5)
    k = l2_normalize(k.reshape(B, L, DN_H, DN_DK))
    v = v.reshape(B, L, DN_H, DN_DV)
    beta = jax.nn.sigmoid(beta_logits.astype(f32))
    g = -jnp.exp(a_log.astype(f32).reshape(2 * DN_H)) * jax.nn.softplus(
        a.astype(f32) + dt_bias.astype(f32).reshape(2 * DN_H))
    o_fwd = gated_delta_chunked(q, k, v, g[..., :DN_H], beta[..., :DN_H])
    o_bwd = reverse_seq(gated_delta_chunked(reverse_seq(q), reverse_seq(k), reverse_seq(v),
                                            reverse_seq(g[..., DN_H:]), reverse_seq(beta[..., DN_H:])))
    o = rms_norm(o_fwd + o_bwd, out_norm_w) * jax.nn.silu(z.astype(f32).reshape(B, L, DN_H, DN_DV))
    return o.reshape(B, L, DN_V).astype(qkv.dtype)

def partial_rope(x):
    L = x.shape[1]
    half = ROPE_DIM // 2
    inv_freq = ROPE_THETA ** (-jnp.arange(half, dtype=jnp.float32) * 2.0 / ROPE_DIM)
    ang = jnp.arange(L, dtype=jnp.float32)[:, None] * inv_freq[None, :]
    cos = jnp.cos(ang)[None, :, None, :].astype(x.dtype)
    sin = jnp.sin(ang)[None, :, None, :].astype(x.dtype)
    x1 = x[..., :half]
    x2 = x[..., half:ROPE_DIM]
    return jnp.concatenate([x1 * cos - x2 * sin, x2 * cos + x1 * sin, x[..., ROPE_DIM:]], axis=-1)

def banded_window_attention(q, k, v, sink):
    B, L, _, _ = q.shape
    G = SWA_HQ // SWA_HKV
    NB = L // BLOCK
    f32 = jnp.float32
    qb = q.reshape(B, NB, BLOCK, SWA_HKV, G, SWA_HD)

    def key_windows(t):
        tp = jnp.pad(t, ((0, 0), (BLOCK, BLOCK), (0, 0), (0, 0))).reshape(B, NB + 2, BLOCK, SWA_HKV, SWA_HD)
        return jnp.concatenate([tp[:, :-2], tp[:, 1:-1], tp[:, 2:]], axis=2)

    kw, vw = key_windows(k), key_windows(v)
    s = jnp.einsum('bnqhgd,bnkhd->bnhgqk', qb, kw).astype(f32) * (SWA_HD ** -0.5)
    qi = jnp.arange(BLOCK)[:, None]
    kj = jnp.arange(3 * BLOCK)[None, :]
    band = jnp.abs(kj - BLOCK - qi) <= WINDOW
    kpos = jnp.arange(NB)[:, None] * BLOCK + jnp.arange(3 * BLOCK)[None, :] - BLOCK
    in_seq = (kpos >= 0) & (kpos < L)
    mask = band[None] & in_seq[:, None, :]
    s = jnp.where(mask[None, :, None, None], s, -jnp.inf)
    sink_logit = jnp.broadcast_to(sink.astype(f32).reshape(1, 1, SWA_HKV, G, 1, 1), s.shape[:-1] + (1,))
    p = jax.nn.softmax(jnp.concatenate([s, sink_logit], axis=-1), axis=-1)[..., :-1]
    o = jnp.einsum('bnhgqk,bnkhd->bnqhgd', p.astype(v.dtype), vw)
    return o.reshape(B, L, SWA_HQ, SWA_HD)

def window_gqa_branch(q, kv, q_norm_w, k_norm_w, sink):
    B, L, _ = q.shape
    q = q.reshape(B, L, SWA_HQ, SWA_HD)
    k, v = split_last(kv, (SWA_HKV * SWA_HD, SWA_HKV * SWA_HD))
    k = k.reshape(B, L, SWA_HKV, SWA_HD)
    v = v.reshape(B, L, SWA_HKV, SWA_HD)
    q = partial_rope(rms_norm(q, q_norm_w))
    k = partial_rope(rms_norm(k, k_norm_w))
    o = banded_window_attention(q, k, v, sink)
    return o.reshape(B, L, SWA_HQ * SWA_HD)

def hybrid_layer(x, c, w_ada, b_ada, norm1_w, w_in, conv_w, dn_a_log, dn_dt_bias, dn_out_norm_w,
                 w_dn_proj, q_norm_w, k_norm_w, sink, w_swa_proj, w_out, norm2_w, w_mlp_in, w_mlp_out):
    mod = jnp.dot(jax.nn.silu(c), w_ada) + b_ada
    shift1, scale1, gate1, shift2, scale2, gate2 = jnp.split(mod[:, None, :], 6, axis=-1)

    h = rms_norm(x, norm1_w) * (1.0 + scale1) + shift1
    proj = jnp.dot(h, w_in)
    qkv_dn, z_dn, beta_dn, a_dn, q_sw, kv_sw, gates = split_last(proj, IN_SIZES)
    y_dn = deltanet_branch(qkv_dn, z_dn, beta_dn, a_dn, conv_w, dn_a_log, dn_dt_bias, dn_out_norm_w)
    y_sw = window_gqa_branch(q_sw, kv_sw, q_norm_w, k_norm_w, sink)
    gate_dn, gate_sw = jnp.split(jax.nn.sigmoid(gates), 2, axis=-1)
    merged = gate_dn * jnp.dot(y_dn, w_dn_proj) + gate_sw * jnp.dot(y_sw, w_swa_proj)
    x = x + gate1 * jnp.dot(merged, w_out)

    h = rms_norm(x, norm2_w) * (1.0 + scale2) + shift2
    u = jnp.square(jax.nn.relu(jnp.dot(h, w_mlp_in)))
    x = x + gate2 * jnp.dot(u, w_mlp_out)
    return x

def setup_inputs(seed: int = 0) -> dict:
    key = jax.random.key(seed)
    ks = jax.random.split(key, 20)
    f32 = jnp.float32

    def dense(k, shape, fan_in):
        return jax.random.normal(k, shape, f32) * (fan_in ** -0.5)

    def gain(k, n):
        return 1.0 + 0.02 * jax.random.normal(k, (DEPTH, n), f32)

    x = jax.random.normal(ks[0], (BATCH, SEQ, D_MODEL), f32)
    c = jax.random.normal(ks[1], (BATCH, D_MODEL), f32)
    w_ada = dense(ks[2], (DEPTH, D_MODEL, 6 * D_MODEL), D_MODEL)
    b_ada = 0.02 * jax.random.normal(ks[3], (DEPTH, 6 * D_MODEL), f32)
    norm1_w = gain(ks[4], D_MODEL)
    w_in = dense(ks[5], (DEPTH, D_MODEL, IN_WIDTH), D_MODEL)
    conv_w = dense(ks[6], (DEPTH, CONV_K, DN_CONV_CH), CONV_K)
    dn_a_log = jnp.log(jax.random.uniform(ks[7], (DEPTH, 2, DN_H), f32, minval=1.0, maxval=16.0))
    dt = jnp.exp(jax.random.uniform(ks[8], (DEPTH, 2, DN_H), f32,
                                    minval=math.log(1e-3), maxval=math.log(1e-1)))
    dn_dt_bias = dt + jnp.log(-jnp.expm1(-dt))
    dn_out_norm_w = gain(ks[9], DN_DV)
    w_dn_proj = dense(ks[10], (DEPTH, DN_V, D_MODEL), DN_V)
    q_norm_w = gain(ks[11], SWA_HD)
    k_norm_w = gain(ks[12], SWA_HD)
    sink = jax.random.normal(ks[13], (DEPTH, SWA_HQ), f32)
    w_swa_proj = dense(ks[14], (DEPTH, SWA_HQ * SWA_HD, D_MODEL), SWA_HQ * SWA_HD)
    w_out = dense(ks[15], (DEPTH, D_MODEL, D_MODEL), D_MODEL)
    norm2_w = gain(ks[16], D_MODEL)
    w_mlp_in = dense(ks[17], (DEPTH, D_MODEL, D_FF), D_MODEL)
    w_mlp_out = dense(ks[18], (DEPTH, D_FF, D_MODEL), D_FF)
    return {"x": x, "c": c, "w_ada": w_ada, "b_ada": b_ada, "norm1_w": norm1_w, "w_in": w_in,
            "conv_w": conv_w, "dn_a_log": dn_a_log, "dn_dt_bias": dn_dt_bias,
            "dn_out_norm_w": dn_out_norm_w, "w_dn_proj": w_dn_proj, "q_norm_w": q_norm_w,
            "k_norm_w": k_norm_w, "sink": sink, "w_swa_proj": w_swa_proj, "w_out": w_out,
            "norm2_w": norm2_w, "w_mlp_in": w_mlp_in, "w_mlp_out": w_mlp_out}

def reference(x, c, w_ada, b_ada, norm1_w, w_in, conv_w, dn_a_log, dn_dt_bias, dn_out_norm_w,
              w_dn_proj, q_norm_w, k_norm_w, sink, w_swa_proj, w_out, norm2_w, w_mlp_in, w_mlp_out):
    for layer in range(DEPTH):
        x = hybrid_layer(x, c, w_ada[layer], b_ada[layer], norm1_w[layer], w_in[layer], conv_w[layer],
                         dn_a_log[layer], dn_dt_bias[layer], dn_out_norm_w[layer], w_dn_proj[layer],
                         q_norm_w[layer], k_norm_w[layer], sink[layer], w_swa_proj[layer],
                         w_out[layer], norm2_w[layer], w_mlp_in[layer], w_mlp_out[layer])
    return x


_drawn_inputs = setup_inputs


def setup_inputs(seed=0):
    import zlib

    import numpy as np

    out = dict(_drawn_inputs(seed))
    spreads = {}
    factors = {'norm1_w': 7.587,
     'dn_out_norm_w': 8.0,
     'q_norm_w': 8.0,
     'k_norm_w': 8.0,
     'sink': 8.0,
     'norm2_w': 15.571}
    for name, (base, spread) in spreads.items():
        noise = np.random.default_rng([zlib.crc32(name.encode()), seed]).standard_normal(out[name].shape)
        drawn = base * np.exp(spread * noise) if base else spread * noise
        out[name] = __import__('jax').numpy.asarray(drawn.astype(out[name].dtype))
    for name, factor in factors.items():
        out[name] = (out[name] * factor).astype(out[name].dtype)
    return out
```

```python
import math
from contextlib import ExitStack

import concourse.bass as bass
from concourse import mybir
import numpy as np

FP32 = mybir.dt.float32
FP32R = mybir.dt.float32r
ACT = mybir.ActivationFunctionType
ALU = mybir.AluOpType
AX = mybir.AxisListType

P = 128
SEQ, D, DFF = 512, 2048, 8192
KT = D // P
HEADS, KV_HEADS = 8, 2
NCH = SEQ // P
CONV_K = 5
EPS = 1e-6
SCALE = float(P) ** -0.5
QKV_T, Z_T = 24, 8
LEVELS = 7

ROWS, COLS = 8, 256
SLOT = ROWS * COLS
SW_BODIES, DN_BODIES, Z_BODIES, OUT_BODIES = 3, 6, 2, 4
MERGE_BLOCKS = D // COLS
CHUNKS = DFF // (ROWS * P)
S_MERGE = 4 * (SW_BODIES + DN_BODIES + Z_BODIES)
S_OUT = S_MERGE + 6 * MERGE_BLOCKS
S_MLP = S_OUT + 4 * OUT_BODIES
N_SLOTS = S_MLP + 16 * CHUNKS
ADA_G = 6 * D // 512
ADA_A, ADA_P1 = 8, 8

C_COL, BADA, N1W, N2W, CONVW = 0, 16, 112, 128, 144
ONW, QNW, KNW, DTB, ALOG, SINK, EPSC, LNS, ONEC = 264, 265, 266, 267, 283, 299, 307, 308, 309
N_PAR = 310
SH1, SC1, GA1, SH2, SC2, GA2 = (KT * n for n in range(6))

M_IDENT, M_LE, M_GE = 0, 1, 2
M_KEEP_T, M_KEEP = 3, 5
M_LVL = 7
M_BAND, M_ROT, M_COS, M_SIN = 21, 24, 25, 29
N_MASK = 33


def masks():
    i = np.arange(P)
    r, c = i[:, None], i[None, :]
    huge = np.float32(1e30)
    m = [r == c, r <= c, r >= c]
    m += [np.where(r <= c, 0, -huge), np.where(r >= c, 0, -huge)]
    m += [np.where(r > c, 0, huge), np.where(r < c, 0, huge)]
    for lvl in range(LEVELS):
        b = 1 << lvl
        low = ((r // b) % 2 == 1) & (c // b == r // b - 1)
        m += [low, low.T]
    m += [np.where(c >= r, 0, -huge), np.zeros((P, P)), np.where(c <= r, 0, -huge)]
    rot = np.zeros((P, P))
    half = P // 8
    for k in range(half):
        rot[half + k, k] = -1.0
        rot[k, half + k] = 1.0
    m.append(rot)
    inv = (np.float32(500000.0) ** (-np.arange(half, dtype=np.float32) * np.float32(2.0) / np.float32(2 * half))).astype(np.float32)
    ang = (np.arange(SEQ, dtype=np.float32)[:, None] * inv[None, :]).astype(np.float32)
    cos, sin = np.zeros((P, SEQ)), np.zeros((P, SEQ))
    cos[:half] = cos[half:2 * half] = np.cos(ang).T
    sin[:half] = sin[half:2 * half] = np.sin(ang).T
    m += [cos, sin]
    return np.ascontiguousarray(np.concatenate([np.asarray(x, np.float32) for x in m], axis=1))


SC_G, SC_GC, SC_BETA, SC_NBE, SC_KD, SC_EGL = range(6)
SP_G, SP_LEFT, SP_DVE_ALL, SP_ACT_ALL = 6, 7, 20, 11


def hybrid_block_kernel(nc, wstream, adastream, wsmall, xT, params, maskc, outT):
    ctx = ExitStack()
    cursor = [16512]

    def size_of(shape):
        return (4 * int(np.prod(shape[1:])) + 31) // 32 * 32

    def lasting(name, shape, dt=FP32):
        t = nc.alloc_sbuf_tensor_at(name, shape, dt, offset=cursor[0])
        cursor[0] += size_of(shape)
        return t

    raw = [lasting(f"raw{b}", [P, SLOT]) for b in range(4)]
    w_hi = [lasting(f"w_hi{b}", [P, SLOT], FP32R) for b in range(2)]
    w_lo = [lasting(f"w_lo{b}", [P, SLOT], FP32R) for b in range(2)]
    act_hi = lasting("act_hi", [P, KT, SEQ], FP32R)
    act_lo = lasting("act_lo", [P, KT, SEQ], FP32R)
    par = lasting("par", [P, N_PAR])
    ones = lasting("ones", [P, P])
    csilu = lasting("csilu", [P, KT])
    mod = lasting("mod", [P, 6 * KT])
    gain = lasting("gain", [P, 2, KT])
    ada_acc = lasting("ada_acc", [P, 512])
    scal = lasting("scal", [P, HEADS, 2, 6, NCH])
    phase_base = cursor[0]

    def phase(start=0):
        where = [phase_base + start]

        def take(name, shape, dt=FP32):
            t = nc.alloc_sbuf_tensor_at(name, shape, dt, offset=where[0])
            where[0] += size_of(shape)
            return t

        return take

    r = phase()
    xs = r("xs", [P, KT, SEQ])
    sq = [r(f"sq{b}", [P, SEQ]) for b in range(2)]
    rstd = r("rstd", [P, SEQ])
    lnb = r("lnb", [P, SEQ])
    scaled = [r(f"scaled{b}", [P, SEQ]) for b in range(4)]
    r = phase()
    xpad = [r(f"xpad{b}", [P, 2, SEQ + CONV_K - 1]) for b in range(2)]
    expo = [r(f"expo{b}", [P, 2, SEQ]) for b in range(2)]
    stg = [r(f"stg{b}", [P, 2, SEQ]) for b in range(2)]
    sp_raw = r("sp_raw", [P, KT * 32])
    sp_hi = r("sp_hi", [P, KT * 32], FP32R)
    sp_lo = r("sp_lo", [P, KT * 32], FP32R)
    tri = r("tri", [P, 2, P])
    logits = r("logits", [P, NCH, 32])
    (e_beta, a_raw, a_abs, a_exp, a_ln, a_soft, g_tok, g_cum, g_sum, g_left, e_cum, e_left, e_sum, nbe) = (
        r(f"s_{n}", [P, NCH, 16]) for n in range(14))
    e_alog = r("e_alog", [P, 16])
    r = phase()
    am = r("am", [P, 12, P])
    a_id = r("a_id", [P, P])
    k_fin = [r(f"k_fin{n}", [P, SEQ]) for n in range(KV_HEADS)]
    v_tok = [r(f"v_tok{n}", [P, NCH, P]) for n in range(KV_HEADS)]
    q_raw = [r(f"q_raw{b}", [P, SEQ]) for b in range(2)]
    v_raw = [r(f"v_raw{b}", [P, SEQ]) for b in range(2)]
    q_sq = r("q_sq", [P, SEQ])
    q_ri = r("q_ri", [P, SEQ])
    q_nrm = r("q_nrm", [P, SEQ])
    rtmp = r("rtmp", [P, SEQ])
    prob = r("prob", [P, NCH, 3 * P])
    prob_t = r("prob_t", [P, NCH, 3 * P])
    s_max, s_neg, s_sum, s_sink, e_sink, s_inv = (r(f"a_{n}", [P, NCH]) for n in range(6))
    a_out = [r(f"a_out{b}", [P, SEQ]) for b in range(2)]
    band, rot_m = am[:, 0:3, :], am[:, 3, :]
    cos_t = am[:, 4:8, :].rearrange("p a n -> p (a n)")
    sin_t = am[:, 8:12, :].rearrange("p a n -> p (a n)")
    r = phase()
    dm = r("dm", [P, M_BAND, P])
    qkv = r("qkv", [P, 3, SEQ])
    z_s = r("z_s", [P, SEQ])
    hs = r("hs", [P, 2, 6, NCH])
    qn = r("qn", [P, SEQ])
    kn = r("kn", [P, SEQ])
    nsq = [r(f"nsq{n}", [P, SEQ]) for n in range(2)]
    k_tok = r("k_tok", [P, NCH, P])
    bv, aT, amat, qd, Tm, Xm, Ym = ([r(f"{n}{d}", [P, NCH, P]) for d in range(2)] for n in ("bv", "aT", "amat", "qd", "Tm", "Xm", "Ym"))
    state, resid, vnew, vdec = ([r(f"{n}{d}", [P, P]) for d in range(2)] for n in ("state", "resid", "vnew", "vdec"))
    o_t = r("o_t", [P, SEQ])
    y_t = r("y_t", [P, SEQ])
    r = phase()
    y_hi = r("y_hi", [P, KT, SEQ], FP32R)
    y_lo = r("y_lo", [P, KT, SEQ], FP32R)
    gA = r("gA", [P, 2, SEQ])
    gB = r("gB", [P, 2, SEQ])
    r = phase(2 * KT * SEQ * 4)
    restg = [r(f"restg{b}", [P, SEQ]) for b in range(4)]
    r = phase(KT * SEQ * 4)
    u_hi = r("u_hi", [P, ROWS, SEQ], FP32R)
    u_lo = r("u_lo", [P, ROWS, SEQ], FP32R)
    urelu = [r(f"urelu{b}", [P, 2, SEQ]) for b in range(2)]

    bank = [ctx.enter_context(nc.psum_tensor(f"bank{n}", [P, 512], FP32)) for n in range(8)]

    def chunked(ap, n=NCH):
        return ap.rearrange("p (c n) -> p c n", c=n)

    def scratch(name, n):
        return nc.dram_tensor(name, [n, P, SEQ], FP32)

    sw_d, dn_d, z_d = scratch("sw_d", 12), scratch("dn_d", QKV_T), scratch("z_d", Z_T)
    y_d, mg_d = scratch("y_d", KT), scratch("mg_d", KT)

    def tiles_of(t, first, n=1):
        return t[bass.ds(first, n)].rearrange("a p n -> p a n")

    def sem(name):
        return ctx.enter_context(nc.semaphore(name))

    def sems(name, n=2):
        return [sem(f"{name}{b}") for b in range(n)]

    raw_full = sems("raw_full", 4)
    par_in, x_in, x_back, mask_in, sp_in, kv_in, dmask_in = (sem(n) for n in ("par_in", "x_in", "x_back", "mask_in", "sp_in", "kv_in", "dmask_in"))
    stg_out, q_in, a_stored = sems("stg_out"), sems("q_in"), sems("a_stored")
    head_in, z_in, y_stored = sem("head_in"), sem("z_in"), sem("y_stored")
    restg_in, mg_stored, out_stored = sems("restg_in", 4), sem("mg_stored"), sem("out_stored")
    hi_done, lo_done, slot_used = sem("hi_done"), sem("lo_done"), sem("slot_used")
    c_exp, c_step = sem("c_exp"), sem("c_step")
    ada_step, ada_summed, mod_done = sem("ada_step"), sem("ada_summed"), sem("mod_done")
    ones_set, pad_set = sem("ones_set"), sem("pad_set")
    sq_done, sq_used, ln_done, rstd_done = (sem(n) for n in ("sq_done", "sq_used", "ln_done", "rstd_done"))
    gain_done, scaled_done, h_hi, h_lo = (sem(n) for n in ("gain_done", "scaled_done", "h_hi", "h_lo"))
    evac, silu_exp, silu_done, conv_step, silu_step = sems("evac"), sem("silu_exp"), sem("silu_done"), sem("conv_step"), sem("silu_step")
    sp_hi_done, sp_lo_done, sp_summed, cums_done, sp_act, sp_dve = (sem(n) for n in ("sp_hi_done", "sp_lo_done", "sp_summed", "cums_done", "sp_act", "sp_dve"))
    aq_sq, aq_summed, aq_ln, aq_rinv, aq_normed, aq_turned, aq_roped, aq_step = (
        sem(n) for n in ("aq_sq", "aq_summed", "aq_ln", "aq_rinv", "aq_normed", "aq_turned", "aq_roped", "aq_step"))
    av_turned, av_copied = sem("av_turned"), sem("av_copied")
    scores_mm, scored, maxed, negated, p_exp, sink_exp, p_step, p_ready = (
        sem(n) for n in ("scores_mm", "scored", "maxed", "negated", "p_exp", "sink_exp", "p_step", "p_ready"))
    p_turned, p_copied, ao_mm, ao_copied = sems("p_turned"), sems("p_copied"), sem("ao_mm"), sem("ao_copied")
    qk_sq, qk_sum, qk_ln, qk_rinv, qk_normed, hs_set = (sem(n) for n in ("qk_sq", "qk_sum", "qk_ln", "qk_rinv", "qk_normed", "hs_set"))
    v_turned, bv_done, k_turned, ktok_done, grams, gb_done = (sem(n) for n in ("v_turned", "bv_done", "k_turned", "ktok_done", "grams", "gb_done"))
    exponents, decays, a_made, t_first, t_made, x_turned, x_copied = (
        sem(n) for n in ("exponents", "decays", "a_made", "t_first", "t_made", "x_turned", "x_copied"))
    y_mm, y_masked, xp_mm, tp_mm, x_upd, t_upd = (sems(n) for n in ("y_mm", "y_masked", "xp_mm", "tp_mm", "x_upd", "t_upd"))
    ks_mm, resid_done, vn_mm, v_copied, kv_mm, state_upd = (sems(n) for n in ("ks_mm", "resid_done", "vn_mm", "v_copied", "kv_mm", "state_upd"))
    o_mm, of_copied, o_sum, o_sq, o_summed, o_ln, o_rinv, o_normed, y_gated = (
        sem(n) for n in ("o_mm", "of_copied", "o_sum", "o_sq", "o_summed", "o_ln", "o_rinv", "o_normed", "y_gated"))
    re_hi, re_lo = sem("re_hi"), sem("re_lo")
    gate_exp, gate_step, gates_done, dn_merged, sw_merged, mg_full = sems("gate_exp"), sem("gate_step"), sem("gates_done"), sem("dn_merged"), sem("sw_merged"), sem("mg_full")
    x1_done = sems("x1_done")
    u_relu, u_sq, u_high, u_ready, y_added = sems("u_relu"), sems("u_sq"), sems("u_high"), sems("u_ready"), sems("y_added", 4)

    block = ctx.enter_context(nc.Block())
    ADA_ALL = ADA_A + ADA_P1 + MERGE_BLOCKS

    @block.sync
    def _(sp):
        sp.dma_start(par[:, :], params).then_inc(par_in, 16)
        sp.dma_start(xs[:, :, :], xT.rearrange("(k p) n -> p k n", p=P)).then_inc(x_in, 16)

        def load(stream, s, b):
            sp.dma_start(raw[b][:, :], stream[bass.ds(s, 1)].rearrange("a p n -> (a p) n")).then_inc(raw_full[b], 16)

        for j in range(4):
            load(adastream, j, j)
        with sp.Fori(1, ADA_A) as g:
            for j in range(4):
                sp.wait_ge(ada_step, g * 16 + 4 * j - 12)
                load(adastream, g * 4 + j, j)
        for j in range(2):
            sp.wait_ge(ada_step, 16 * ADA_A - 12 + 4 * j)
            load(wstream, j, j)

        def load_w(s, b):
            sp.wait_ge(lo_done, s - 1)
            load(wstream, s, b)

        def load_ada(g, j):
            sp.wait_ge(ada_step, g * 16 + 4 * j - 4)
            load(adastream, g * 4 + j, 2 + j % 2)

        with sp.Fori(0, SW_BODIES) as i:
            for j in range(4):
                load_w(i * 4 + 2 + j, j % 2)
        with sp.Fori(0, DN_BODIES + Z_BODIES) as i:
            for j in range(4):
                load_w(i * 4 + 4 * SW_BODIES + 2 + j, j % 2)
                load_ada(i + ADA_A, j)
        with sp.Fori(0, MERGE_BLOCKS) as i:
            for j in range(6):
                load_w(i * 6 + S_MERGE + 2 + j, j % 2)
                if j < 4:
                    load_ada(i + ADA_A + ADA_P1, j)
        with sp.Fori(0, (N_SLOTS - S_OUT - 2) // 2) as i:
            for j in range(2):
                load_w(i * 2 + S_OUT + 2 + j, j)
        sp.wait_ge(out_stored, 16 * MERGE_BLOCKS)

    @block.gpsimd
    def _(pool):
        pool.memset(ones[:, :], 1.0).then_inc(ones_set, 1)
        pool.wait_ge(h_hi, KT)
        pool.wait_ge(h_lo, KT)
        for b in range(2):
            pool.memset(xpad[b][:, :, :], 0.0).then_inc(pad_set, 1)
        pool.dma_start(sp_raw[:, :], wsmall).then_inc(sp_in, 16)
        pool.dma_start(tri[:, :, :], chunked(maskc[:, P * M_LE:P * (M_GE + 1)], 2)).then_inc(sp_in, 16)

        with pool.Fori(0, SW_BODIES) as i:
            for b in range(2):
                pool.wait_ge(evac[b], i + 1)
                pool.dma_start(tiles_of(sw_d, i * 4 + 2 * b, 2), stg[b][:, :, :]).then_inc(stg_out[b], 16)
        with pool.Fori(0, DN_BODIES) as i:
            for b in range(2):
                pool.wait_ge(silu_done, i * 2 + b + 1)
                pool.dma_start(tiles_of(dn_d, i * 4 + 2 * b, 2), stg[b][:, :, :]).then_inc(stg_out[b], 16)
        with pool.Fori(0, Z_BODIES) as i:
            for b in range(2):
                pool.wait_ge(silu_done, i * 2 + 2 * DN_BODIES + b + 1)
                pool.dma_start(tiles_of(z_d, i * 4 + 2 * b, 2), stg[b][:, :, :]).then_inc(stg_out[b], 16)

        pool.wait_ge(sp_dve, SP_DVE_ALL)
        pool.wait_ge(sp_act, SP_ACT_ALL)
        for b in range(2):
            pool.wait_ge(stg_out[b], 16 * (SW_BODIES + DN_BODIES + Z_BODIES))
        pool.dma_start(am[:, :, :], chunked(maskc[:, P * M_BAND:], 12)).then_inc(mask_in, 16)
        pool.dma_start(a_id[:, :], maskc[:, 0:P]).then_inc(mask_in, 16)
        for n in range(KV_HEADS):
            pool.dma_start(q_raw[n][:, :], sw_d[HEADS + n]).then_inc(kv_in, 16)
            pool.dma_start(v_raw[n][:, :], sw_d[HEADS + KV_HEADS + n]).then_inc(kv_in, 16)
        for b in range(2):
            pool.wait_ge(aq_normed, b + 1)
            pool.dma_start(q_raw[b][:, :], sw_d[b]).then_inc(q_in[b], 16)
        with pool.Fori(0, HEADS // 2 - 1) as i:
            for b in range(2):
                pool.wait_ge(aq_normed, i * 2 + KV_HEADS + b + 1)
                pool.dma_start(q_raw[b][:, :].unsqueeze(1), tiles_of(sw_d, i * 2 + 2 + b)).then_inc(q_in[b], 16)
                pool.wait_ge(ao_copied, i * 2 + b + 1)
                pool.dma_start(tiles_of(y_d, i * 2 + HEADS + b), a_out[b][:, :].unsqueeze(1)).then_inc(a_stored[b], 16)
        for b in range(2):
            pool.wait_ge(ao_copied, HEADS - 1 + b)
            pool.dma_start(y_d[2 * HEADS - 2 + b], a_out[b][:, :]).then_inc(a_stored[b], 16)

        for b in range(2):
            pool.wait_ge(a_stored[b], 16 * (HEADS // 2))
        pool.dma_start(dm[:, :, :], chunked(maskc[:, 0:P * M_BAND], M_BAND)).then_inc(dmask_in, 16)

        def load_head(h):
            for n in range(3):
                pool.dma_start(qkv[:, n:n + 1, :], tiles_of(dn_d, h + HEADS * n)).then_inc(head_in, 16)

        load_head(0)
        pool.dma_start(z_s[:, :], z_d[0]).then_inc(z_in, 16)
        with pool.Fori(0, HEADS - 1) as h:
            pool.wait_ge(qk_normed, h * 2 + 2)
            pool.wait_ge(v_turned, h + 1)
            load_head(h + 1)
            pool.wait_ge(y_gated, h + 1)
            pool.dma_start(tiles_of(y_d, h), y_t[:, :].unsqueeze(1)).then_inc(y_stored, 16)
            pool.dma_start(z_s[:, :].unsqueeze(1), tiles_of(z_d, h + 1)).then_inc(z_in, 16)
        pool.wait_ge(y_gated, HEADS)
        pool.dma_start(y_d[HEADS - 1], y_t[:, :]).then_inc(y_stored, 16)
        pool.wait_ge(y_stored, 16 * HEADS)

        def restage(src, base):
            for k in range(KT):
                if base + k >= 4:
                    pool.wait_ge(re_lo, base + k - 3)
                pool.dma_start(restg[k % 4][:, :], src[k]).then_inc(restg_in[k % 4], 16)

        restage(y_d, 0)
        with pool.Fori(0, MERGE_BLOCKS) as i:
            pool.wait_ge(mg_full, i + 1)
            pool.dma_start(tiles_of(mg_d, i * 2, 2), gA[:, :, :]).then_inc(mg_stored, 16)
        pool.wait_ge(mg_stored, 16 * MERGE_BLOCKS)
        pool.wait_ge(slot_used, S_OUT)
        pool.dma_start(xs[:, :, :], xT.rearrange("(k p) n -> p k n", p=P)).then_inc(x_back, 16)
        restage(mg_d, KT)
        for j in range(MERGE_BLOCKS):
            pool.wait_ge(y_added[j % 4], 2 * CHUNKS - 1 + j // 4)
            pool.dma_start(outT[2 * j * P:2 * (j + 1) * P, :].rearrange("(a p) n -> p a n", p=P), xs[:, 2 * j:2 * j + 2, :]).then_inc(out_stored, 16)

    SPLIT_FREE = 16 * (ADA_A + 1)

    @block.scalar
    def _(act):
        eps = par[:, EPSC:EPSC + 1]

        def split_hi(s, b):
            act.wait_ge(raw_full[b], (s - b) * 8 + SPLIT_FREE)
            act.wait_ge(slot_used, s - 1)
            act.activation(w_hi[b][:, :], raw[b][:, :], ACT.Copy).then_inc(hi_done, 1)

        def norm(n):
            for k in range(KT):
                if k >= 2 or n:
                    act.wait_ge(sq_used, KT * n + k - 1)
                act.activation(sq[k % 2][:, :], xs[:, k, :], ACT.Square).then_inc(sq_done, 1)
            act.wait_ge(sq_used, KT * (n + 1))
            act.activation(lnb[:, :], bank[0][:, :], ACT.Ln, bias=eps, scale=1.0 / D).then_inc(ln_done, 1)
            act.wait_ge(ln_done, n + 1)
            act.activation(rstd[:, :], lnb[:, :], ACT.Exp, scale=-0.5).then_inc(rstd_done, 1)
            shift = (SH1, SH2)[n]
            for k in range(KT):
                act.wait_ge(scaled_done, KT * n + k + 1)
                act.activation(act_hi[:, k, :], scaled[k % 4][:, :], ACT.Identity, bias=mod[:, shift + k:shift + k + 1]).then_inc(h_hi, 1)

        act.wait_ge(par_in, 16)
        act.activation(csilu[:, :], par[:, C_COL:C_COL + KT], ACT.Exp, scale=-1.0).then_inc(c_exp, 1)
        act.wait_ge(x_in, 16)
        norm(0)
        for b in range(2):
            act.wait_ge(raw_full[b], SPLIT_FREE)
            act.activation(w_hi[b][:, :], raw[b][:, :], ACT.Copy).then_inc(hi_done, 1)

        act.wait_ge(h_lo, KT)
        act.wait_ge(pad_set, 2)

        def block_out(i, first, b, dst):
            act.wait_ge(slot_used, i * 4 + (4 * first + 2 * b + 2))
            for t in range(2):
                last = act.activation(dst[:, t, :], bank[2 * b + t][:, :], ACT.Copy)
            last.then_inc(evac[b], 1)

        with act.Fori(0, SW_BODIES) as i:
            for b in range(2):
                split_hi(i * 4 + (2 + 2 * b), 0)
                act.wait_ge(stg_out[b], i * 16)
                block_out(i, 0, b, stg[b])
                split_hi(i * 4 + (3 + 2 * b), 1)
        with act.Fori(0, DN_BODIES) as i:
            for b in range(2):
                split_hi(i * 4 + (4 * SW_BODIES + 2 + 2 * b), 0)
                act.wait_ge(silu_done, i * 2)
                block_out(i, SW_BODIES, b, xpad[b][:, :, 2:2 + SEQ])
                split_hi(i * 4 + (4 * SW_BODIES + 3 + 2 * b), 1)
                act.wait_ge(conv_step, i * 20 + (b + 1) * 10)
                act.activation(expo[b][:, :, :], stg[b][:, :, :], ACT.Exp, scale=-1.0).then_inc(silu_exp, 1)
        with act.Fori(0, Z_BODIES) as i:
            for b in range(2):
                first = SW_BODIES + DN_BODIES
                split_hi(i * 4 + (4 * first + 2 + 2 * b), 0)
                act.wait_ge(silu_done, i * 2 + (2 * DN_BODIES))
                block_out(i, first, b, xpad[b][:, :, 2:2 + SEQ])
                act.wait_ge(evac[b], i + (first + 1))
                act.activation(expo[b][:, :, :], xpad[b][:, :, 2:2 + SEQ], ACT.Exp, scale=-1.0).then_inc(silu_exp, 1)
                split_hi(i * 4 + (4 * first + 3 + 2 * b), 1)

        act.wait_ge(sp_in, 32)
        act.activation(sp_hi[:, :], sp_raw[:, :], ACT.Copy).then_inc(sp_hi_done, 1)
        act.activation(e_alog[:, :], par[:, ALOG:ALOG + 16], ACT.Exp).then_inc(sp_act, 1)
        act.wait_ge(sp_summed, 1)
        act.activation(logits[:, :, :], chunked(bank[4][:, 0:NCH * 32]), ACT.Copy).then_inc(sp_act, 1)
        act.wait_ge(sp_act, 2)
        act.activation(e_beta[:, :, :], logits[:, :, 0:16], ACT.Exp, scale=-1.0).then_inc(sp_act, 1)
        act.wait_ge(sp_dve, 2)
        act.activation(a_exp[:, :, :], a_abs[:, :, :], ACT.Exp, scale=-1.0).then_inc(sp_act, 1)
        act.wait_ge(sp_act, 4)
        act.activation(a_ln[:, :, :], a_exp[:, :, :], ACT.Ln, bias=par[:, ONEC:ONEC + 1]).then_inc(sp_act, 1)
        act.wait_ge(cums_done, 1)
        for d in range(2):
            act.activation(g_cum[:, :, 8 * d:8 * d + 8], chunked(bank[5][:, 64 * d:64 * d + 64])[:, :, 8 * d:8 * d + 8], ACT.Copy).then_inc(sp_act, 1)
        act.activation(g_sum[:, :, :], chunked(bank[5][:, 128:192]), ACT.Copy).then_inc(sp_act, 1)
        act.wait_ge(sp_act, 8)
        act.activation(e_cum[:, :, :], g_cum[:, :, :], ACT.Exp).then_inc(sp_act, 1)
        act.activation(e_sum[:, :, :], g_sum[:, :, :], ACT.Exp).then_inc(sp_act, 1)
        act.wait_ge(sp_dve, SP_LEFT)
        act.activation(e_left[:, :, :], g_left[:, :, :], ACT.Exp).then_inc(sp_act, 1)

        def inverse_rms(n, scale=1.0 / P):
            act.wait_ge(aq_summed, n + 1)
            act.activation(q_ri[:, :], bank[0][:, :], ACT.Ln, bias=eps, scale=scale).then_inc(aq_ln, 1)
            act.wait_ge(aq_ln, n + 1)
            act.activation(q_ri[:, :], q_ri[:, :], ACT.Exp, scale=-0.5).then_inc(aq_rinv, 1)

        act.wait_ge(mask_in, 32)
        act.wait_ge(kv_in, 32 * KV_HEADS)
        for n in range(KV_HEADS):
            act.activation(q_sq[:, :], q_raw[n][:, :], ACT.Square).then_inc(aq_sq, 1)
            act.wait_ge(aq_normed, n)
            inverse_rms(n)
            act.wait_ge(av_turned, n + 1)
            act.activation(v_tok[n][:, :, :], chunked(bank[2 + n][:, :]), ACT.Copy).then_inc(av_copied, 1)

        for kv in range(KV_HEADS):
            with act.Fori(0, 2) as i:
                for b in range(2):
                    h = i * 2 + (4 * kv + b)
                    act.wait_ge(q_in[b], i * 16 + (32 * kv + 16))
                    act.activation(q_sq[:, :], q_raw[b][:, :], ACT.Square).then_inc(aq_sq, 1)
                    act.wait_ge(aq_normed, h + KV_HEADS)
                    inverse_rms(h + KV_HEADS)
                    act.wait_ge(negated, h + 1)
                    for c in range(NCH):
                        act.activation(prob[:, c, :], prob[:, c, :], ACT.Exp, bias=s_neg[:, c:c + 1], accum_out=s_sum[:, c:c + 1]).then_inc(p_exp, 1)
                    act.wait_ge(p_step, h * 3 + 1)
                    act.activation(e_sink[:, :], s_sink[:, :], ACT.Exp).then_inc(sink_exp, 1)
                    act.wait_ge(ao_mm, h + 1)
                    act.wait_ge(a_stored[b], i * 16 + 32 * kv)
                    act.activation(a_out[b][:, :], bank[1][:, :], ACT.Copy).then_inc(ao_copied, 1)

        act.wait_ge(dmask_in, 16)
        with act.Fori(0, HEADS) as h:
            act.wait_ge(head_in, h * 48 + 48)
            act.wait_ge(o_summed, h)
            act.activation(nsq[0][:, :], qkv[:, 0, :], ACT.Square).then_inc(qk_sq, 1)
            act.wait_ge(o_normed, h)
            act.activation(nsq[1][:, :], qkv[:, 1, :], ACT.Square).then_inc(qk_sq, 1)
            for k in range(2):
                act.wait_ge(qk_sum, h * 2 + k + 1)
                act.activation(nsq[k][:, :], bank[k][:, :], ACT.Ln, bias=eps).then_inc(qk_ln, 1)
                act.wait_ge(qk_ln, h * 2 + k + 1)
                if k == 0:
                    act.activation(nsq[k][:, :], nsq[k][:, :], ACT.Exp, scale=-0.5, bias=par[:, LNS:LNS + 1]).then_inc(qk_rinv, 1)
                else:
                    act.activation(nsq[k][:, :], nsq[k][:, :], ACT.Exp, scale=-0.5).then_inc(qk_rinv, 1)
            act.wait_ge(v_turned, h + 1)
            act.wait_ge(hs_set, h + 1)
            for d in range(2):
                for c in range(NCH):
                    last = act.activation(bv[d][:, c, :], bank[3][:, c * P:(c + 1) * P], ACT.Copy, scale=hs[:, d, SC_BETA, c:c + 1])
            last.then_inc(bv_done, 1)
            act.wait_ge(k_turned, h + 1)
            act.activation(k_tok[:, :, :], chunked(bank[2][:, :]), ACT.Copy).then_inc(ktok_done, 1)
            for d in range(2):
                act.wait_ge(exponents, h * 2 + d + 1)
                act.activation(aT[d][:, :, :], aT[d][:, :, :], ACT.Exp)
                act.activation(amat[d][:, :, :], amat[d][:, :, :], ACT.Exp, scale=-1.0)
                act.activation(qd[d][:, :, :], chunked(bank[2 + d][:, :]), ACT.Exp).then_inc(decays, 1)
            for d in range(2):
                act.wait_ge(x_turned, h * 2 + d + 1)
                act.activation(Xm[d][:, :, :], chunked(bank[2 + d][:, :]), ACT.Copy).then_inc(x_copied, 1)
            for s in range(NCH):
                for d in range(2):
                    c = s if d == 0 else NCH - 1 - s
                    act.wait_ge(vn_mm[d], h * NCH + s + 1)
                    act.activation(vnew[d][:, :], bank[4 + d][:, P:2 * P], ACT.Copy)
                    act.activation(vdec[d][:, :], bank[4 + d][:, P:2 * P], ACT.Copy, scale=hs[:, d, SC_KD, c:c + 1]).then_inc(v_copied[d], 1)
            act.wait_ge(o_mm, h + 1)
            act.activation(o_t[:, :], bank[6][:, :], ACT.Copy).then_inc(of_copied, 1)
            act.wait_ge(o_sum, h + 1)
            act.activation(nsq[0][:, :], o_t[:, :], ACT.Square).then_inc(o_sq, 1)
            act.wait_ge(o_summed, h + 1)
            act.activation(nsq[1][:, :], bank[4][:, :], ACT.Ln, bias=eps, scale=1.0 / P).then_inc(o_ln, 1)
            act.wait_ge(o_ln, h + 1)
            act.activation(nsq[1][:, :], nsq[1][:, :], ACT.Exp, scale=-0.5).then_inc(o_rinv, 1)

        def restage_hi(dst, base):
            for k in range(KT):
                act.wait_ge(restg_in[k % 4], 16 * ((base + k) // 4 + 1))
                act.activation(dst[:, k, :], restg[k % 4][:, :], ACT.Copy).then_inc(re_hi, 1)

        restage_hi(y_hi, 0)
        act.wait_ge(re_lo, KT)
        with act.Fori(0, MERGE_BLOCKS) as i:
            for g, buf in enumerate((gA, gB)):
                split_hi(i * 6 + (S_MERGE + 2 + 2 * g), 0)
                act.wait_ge(slot_used, i * 6 + (S_MERGE + 2 * g + 2))
                act.wait_ge(mg_full, i)
                if g == 0:
                    act.wait_ge(mg_stored, i * 16)
                for t in range(2):
                    last = act.activation(buf[:, t, :], bank[2 * g + t][:, :], ACT.Exp, scale=-1.0)
                last.then_inc(gate_exp[g], 1)
                split_hi(i * 6 + (S_MERGE + 3 + 2 * g), 1)
            for j in range(2):
                split_hi(i * 6 + (S_MERGE + 6 + j), j)

        act.wait_ge(slot_used, S_OUT)
        restage_hi(act_hi, KT)
        with act.Fori(0, OUT_BODIES) as i:
            for j in range(4):
                split_hi(i * 4 + (S_OUT + 2 + j), j % 2)
        for b in range(2):
            act.wait_ge(x1_done[b], OUT_BODIES)
        norm(1)

        def mlp_in(c):
            with act.Fori(0, 2) as i:
                for b in range(2):
                    split_hi(c * 16 + i * 4 + (S_MLP + 2 + 2 * b), 0)
                    act.wait_ge(slot_used, c * 16 + i * 4 + (S_MLP + 2 * b + 2))
                    act.wait_ge(u_ready[b], c * 2 + i)
                    for t in range(2):
                        last = act.activation(urelu[b][:, t, :], bank[2 * b + t][:, :], ACT.Relu)
                    last.then_inc(u_relu[b], 1)
                    act.wait_ge(u_sq[b], c * 2 + i + 1)
                    act.activation(u_hi[:, bass.ds(i * 4 + 2 * b, 2), :], urelu[b][:, :, :], ACT.Copy).then_inc(u_high[b], 1)
                    split_hi(c * 16 + i * 4 + (S_MLP + 3 + 2 * b), 1)

        with act.Fori(0, CHUNKS - 1) as c:
            mlp_in(c)
            with act.Fori(0, 2) as i:
                for j in range(4):
                    split_hi(c * 16 + i * 4 + (S_MLP + 10 + j), j % 2)
        mlp_in(CHUNKS - 1)
        for j in range(6):
            split_hi(16 * (CHUNKS - 1) + S_MLP + 10 + j, j % 2)

    @block.vector
    def _(dve):
        def split_lo(s, b):
            dve.wait_ge(hi_done, s + 1)
            dve.tensor_tensor(w_lo[b][:, :], raw[b][:, :], w_hi[b][:, :].bitcast(FP32), ALU.subtract).then_inc(lo_done, 1)

        def ada_slot(g, j, b, landed):
            dve.wait_ge(raw_full[b], landed)
            if j == 0:
                dve.wait_ge(ada_summed, g)
            for k in range(4):
                m = 4 * j + k
                src = raw[b][:, k * 512:(k + 1) * 512]
                if m == 0:
                    dve.tensor_scalar(ada_acc[:, :], src, csilu[:, 0:1], None, ALU.mult).then_inc(ada_step, 1)
                else:
                    dve.wait_ge(ada_step, g * 16 + m)
                    dve.scalar_tensor_tensor(out=ada_acc[:, :], in0=src, scalar=csilu[:, m:m + 1], in1=ada_acc[:, :], op0=ALU.mult, op1=ALU.add).then_inc(ada_step, 1)

        def ada_finish(g, sums):
            dve.wait_ge(ada_summed, g + 1)
            dve.tensor_tensor(mod[:, bass.ds(g * 4, 4)], sums, par[:, bass.ds(g * 4 + BADA, 4)], ALU.add).then_inc(mod_done, 1)

        def norm(n):
            nw, scale, shift = ((N1W, SC1, SH1), (N2W, SC2, SH2))[n]
            dve.scalar_tensor_tensor(out=gain[:, n, :], in0=mod[:, scale:scale + KT], scalar=1.0, in1=par[:, nw:nw + KT], op0=ALU.add, op1=ALU.mult).then_inc(gain_done, 1)
            dve.wait_ge(gain_done, n + 1)
            dve.wait_ge(rstd_done, n + 1)
            for k in range(KT + 1):
                if k < KT:
                    if k >= 4:
                        dve.wait_ge(h_lo, KT * n + k - 3)
                    dve.scalar_tensor_tensor(out=scaled[k % 4][:, :], in0=xs[:, k, :], scalar=gain[:, n, k:k + 1], in1=rstd[:, :], op0=ALU.mult, op1=ALU.mult).then_inc(scaled_done, 1)
                if k:
                    j = k - 1
                    dve.wait_ge(h_hi, KT * n + j + 1)
                    dve.scalar_tensor_tensor(out=act_lo[:, j, :], in0=scaled[j % 4][:, :], scalar=mod[:, shift + j:shift + j + 1], in1=act_hi[:, j, :].bitcast(FP32), op0=ALU.add, op1=ALU.subtract).then_inc(h_lo, 1)

        dve.wait_ge(par_in, 16)
        dve.wait_ge(c_exp, 1)
        dve.tensor_scalar(csilu[:, :], csilu[:, :], 1.0, None, ALU.add).then_inc(c_step, 1)
        dve.wait_ge(c_step, 1)
        dve.reciprocal(csilu[:, :], csilu[:, :]).then_inc(c_step, 1)
        dve.wait_ge(c_step, 2)
        dve.tensor_tensor(csilu[:, :], csilu[:, :], par[:, C_COL:C_COL + KT], ALU.mult).then_inc(c_step, 1)
        dve.wait_ge(c_step, 3)
        with dve.Fori(0, ADA_A) as g:
            for j in range(4):
                ada_slot(g, j, j, g * 16 + 16)
            ada_finish(g, bank[7][:, 0:4])
        dve.wait_ge(mod_done, ADA_A)
        dve.wait_ge(x_in, 16)
        norm(0)
        for b in range(2):
            split_lo(b, b)

        def ada_beside(g, j):
            ada_slot(g, j, 2 + j % 2, (g - ADA_A) * 32 + 16 * (ADA_A + 1 + j // 2))

        def silu(n, b, x):
            dve.wait_ge(silu_exp, n + 1)
            dve.tensor_scalar(expo[b][:, :, :], expo[b][:, :, :], 1.0, None, ALU.add).then_inc(silu_step, 1)
            dve.wait_ge(silu_step, n * 2 + 1)
            dve.reciprocal(expo[b][:, :, :], expo[b][:, :, :]).then_inc(silu_step, 1)
            dve.wait_ge(silu_step, n * 2 + 2)
            dve.tensor_tensor(stg[b][:, :, :], expo[b][:, :, :], x, ALU.mult).then_inc(silu_done, 1)

        with dve.Fori(0, SW_BODIES) as i:
            for j in range(4):
                split_lo(i * 4 + (2 + j), j % 2)
        with dve.Fori(0, DN_BODIES) as i:
            for b in range(2):
                for j in range(2):
                    split_lo(i * 4 + (4 * SW_BODIES + 2 + 2 * b + j), j)
                    ada_beside(i + ADA_A, 2 * b + j)
                dve.wait_ge(evac[b], i + (SW_BODIES + 1))
                dve.wait_ge(stg_out[b], i * 16 + 16 * SW_BODIES)
                for k in range(CONV_K):
                    for t in range(2):
                        tap = par[:, bass.ds(i * 20 + (CONVW + (2 * b + t) * CONV_K + k), 1)]
                        src = xpad[b][:, t, k:k + SEQ]
                        if k == 0:
                            dve.tensor_scalar(stg[b][:, t, :], src, tap, None, ALU.mult).then_inc(conv_step, 1)
                        else:
                            dve.wait_ge(conv_step, i * 20 + (10 * b + 2 * k + t - 1))
                            dve.scalar_tensor_tensor(out=stg[b][:, t, :], in0=src, scalar=tap, in1=stg[b][:, t, :], op0=ALU.mult, op1=ALU.add).then_inc(conv_step, 1)
                silu(i * 2 + b, b, stg[b][:, :, :])
            ada_finish(i + ADA_A, bank[7][:, 0:4])
        with dve.Fori(0, Z_BODIES) as i:
            for b in range(2):
                for j in range(2):
                    split_lo(i * 4 + (4 * (SW_BODIES + DN_BODIES) + 2 + 2 * b + j), j)
                    ada_beside(i + (ADA_A + DN_BODIES), 2 * b + j)
                dve.wait_ge(stg_out[b], i * 16 + 16 * (SW_BODIES + DN_BODIES))
                silu(i * 2 + (2 * DN_BODIES + b), b, xpad[b][:, :, 2:2 + SEQ])
            ada_finish(i + (ADA_A + DN_BODIES), bank[7][:, 0:4])

        n_sp = [0]

        def kept(ins):
            n_sp[0] += 1
            ins.then_inc(sp_dve, 1)

        dve.wait_ge(sp_hi_done, 1)
        dve.tensor_tensor(sp_lo[:, :], sp_raw[:, :], sp_hi[:, :].bitcast(FP32), ALU.subtract).then_inc(sp_lo_done, 1)
        dve.wait_ge(sp_act, 2)
        kept(dve.tensor_tensor(a_raw[:, :, :], logits[:, :, 16:32], par[:, DTB:DTB + 16].unsqueeze(1).to_broadcast([P, NCH, 16]), ALU.add))
        dve.wait_ge(sp_dve, 1)
        kept(dve.scalar_tensor_tensor(out=a_abs[:, :, :], in0=a_raw[:, :, :], scalar=-1.0, in1=a_raw[:, :, :], op0=ALU.mult, op1=ALU.max))
        dve.wait_ge(sp_act, 3)
        kept(dve.tensor_scalar(e_beta[:, :, :], e_beta[:, :, :], 1.0, None, ALU.add))
        dve.wait_ge(sp_dve, 3)
        kept(dve.reciprocal(e_beta[:, :, :], e_beta[:, :, :]))
        dve.wait_ge(sp_act, 5)
        kept(dve.scalar_tensor_tensor(out=a_soft[:, :, :], in0=a_raw[:, :, :], scalar=0.0, in1=a_ln[:, :, :], op0=ALU.max, op1=ALU.add))
        dve.wait_ge(sp_dve, 5)
        kept(dve.scalar_tensor_tensor(out=g_tok[:, :, :], in0=a_soft[:, :, :], scalar=-1.0, in1=e_alog[:, :].unsqueeze(1).to_broadcast([P, NCH, 16]), op0=ALU.mult, op1=ALU.mult))
        assert n_sp[0] == SP_G
        dve.wait_ge(sp_act, 8)
        kept(dve.tensor_tensor(g_left[:, :, :], g_sum[:, :, :], g_cum[:, :, :], ALU.subtract))
        assert n_sp[0] == SP_LEFT
        dve.wait_ge(sp_act, 10)
        dve.wait_ge(sp_dve, 4)
        kept(dve.scalar_tensor_tensor(out=nbe[:, :, :], in0=e_cum[:, :, :], scalar=-1.0, in1=e_beta[:, :, :], op0=ALU.mult, op1=ALU.mult))
        dve.wait_ge(sp_act, SP_ACT_ALL)
        dve.wait_ge(sp_dve, n_sp[0])
        for kind, src in ((SC_G, g_tok), (SC_GC, g_cum), (SC_BETA, e_beta), (SC_NBE, nbe), (SC_KD, e_left), (SC_EGL, e_sum)):
            for d in range(2):
                kept(dve.tensor_copy(scal[:, :, d, kind, :], src[:, :, 8 * d:8 * d + 8].rearrange("p c h -> p h c")))
        assert n_sp[0] == SP_DVE_ALL

        def norm_and_rotate(n, src, weight, out):
            dve.wait_ge(aq_rinv, n + 1)
            dve.scalar_tensor_tensor(out=out[:, :], in0=src[:, :], scalar=par[:, weight:weight + 1], in1=q_ri[:, :], op0=ALU.mult, op1=ALU.mult).then_inc(aq_normed, 1)
            dve.wait_ge(aq_turned, n + 1)
            q = 2 * (P // 8)
            dve.tensor_tensor(rtmp[0:q, :], bank[1][0:q, :], sin_t[0:q, :], ALU.mult).then_inc(aq_step, 1)
            dve.tensor_tensor(out[0:q, :], out[0:q, :], cos_t[0:q, :], ALU.mult).then_inc(aq_step, 1)
            dve.wait_ge(aq_step, n * 2 + 2)
            dve.tensor_tensor(out[0:q, :], out[0:q, :], rtmp[0:q, :], ALU.add).then_inc(aq_roped, 1)

        dve.wait_ge(mask_in, 32)
        for n in range(KV_HEADS):
            norm_and_rotate(n, q_raw[n], KNW, k_fin[n])
        for kv in range(KV_HEADS):
            with dve.Fori(0, 2) as i:
                for b in range(2):
                    h = i * 2 + (4 * kv + b)
                    dve.wait_ge(scores_mm, h)
                    norm_and_rotate(h + KV_HEADS, q_raw[b], QNW, q_nrm)
                    for c in range(NCH):
                        dve.wait_ge(scores_mm, h + 1)
                        lo, hi = (P if c == 0 else 0), (2 * P if c == NCH - 1 else 3 * P)
                        dve.scalar_tensor_tensor(out=prob[:, c, lo:hi], in0=bank[4 + c][:, lo:hi], scalar=SCALE, in1=am[:, lo // P:hi // P, :].rearrange("p a n -> p (a n)"), op0=ALU.mult, op1=ALU.add).then_inc(scored, 1)
                    for c in (0, NCH - 1):
                        off = 0 if c == 0 else 2 * P
                        dve.memset(prob[:, c, off:off + P], -1e30).then_inc(scored, 1)
                    dve.wait_ge(scored, h * 6 + 6)
                    dve.tensor_reduce(s_max[:, :], prob[:, :, :], axis=AX.X, op=ALU.max).then_inc(maxed, 1)
                    dve.wait_ge(maxed, h + 1)
                    sink = par[:, bass.ds(SINK + h, 1)]
                    dve.tensor_scalar(s_neg[:, :], s_max[:, :], sink, -1.0, ALU.max, ALU.mult).then_inc(negated, 1)
                    dve.wait_ge(negated, h + 1)
                    dve.tensor_scalar(s_sink[:, :], s_neg[:, :], sink, None, ALU.add).then_inc(p_step, 1)
                    dve.wait_ge(sink_exp, h + 1)
                    dve.wait_ge(p_exp, h * NCH + NCH)
                    dve.tensor_tensor(s_inv[:, :], s_sum[:, :], e_sink[:, :], ALU.add).then_inc(p_step, 1)
                    dve.wait_ge(p_step, h * 3 + 2)
                    dve.reciprocal(s_inv[:, :], s_inv[:, :]).then_inc(p_step, 1)
                    dve.wait_ge(p_step, h * 3 + 3)
                    for c in range(NCH):
                        dve.tensor_scalar(prob[:, c, :], prob[:, c, :], s_inv[:, c:c + 1], None, ALU.mult).then_inc(p_ready, 1)
                    for c in range(NCH):
                        dve.wait_ge(p_turned[c % 2], h * 2 + c // 2 + 1)
                        dve.tensor_copy(prob_t[:, c, :], bank[2 + c % 2][:, 0:3 * P]).then_inc(p_copied[c % 2], 1)

        dve.wait_ge(dmask_in, 16)

        def every(m):
            return dm[:, m, :].unsqueeze(1).to_broadcast([P, NCH, P])

        with dve.Fori(0, HEADS) as h:
            dve.tensor_copy(hs[:, :, :, :].rearrange("p d k c -> p (d k c)"), scal[:, bass.ds(h, 1), :, :, :].rearrange("p h d k c -> p (h d k c)")).then_inc(hs_set, 1)
            for k, dst in enumerate((qn, kn)):
                dve.wait_ge(qk_rinv, h * 2 + k + 1)
                dve.tensor_tensor(dst[:, :], qkv[:, k, :], nsq[k][:, :], ALU.mult).then_inc(qk_normed, 1)
            dve.wait_ge(hs_set, h + 1)
            for d in range(2):
                dve.wait_ge(gb_done, h * 2 + d + 1)
                for c in range(NCH):
                    for out, keep in ((aT[d], M_KEEP_T + d), (amat[d], M_KEEP + d)):
                        last = dve.scalar_tensor_tensor(out=out[:, c, :], in0=bank[2 + d][:, c * P:(c + 1) * P], scalar=hs[:, d, SC_GC, c:c + 1], in1=dm[:, keep, :], op0=ALU.subtract, op1=ALU.add)
                last.then_inc(exponents, 1)
            dve.wait_ge(grams, h + 1)
            for d in range(2):
                dve.wait_ge(decays, h * 2 + d + 1)
                for c in range(NCH):
                    last = dve.scalar_tensor_tensor(out=amat[d][:, c, :], in0=bank[0][:, c * P:(c + 1) * P], scalar=hs[:, d, SC_BETA, c:c + 1], in1=amat[d][:, c, :], op0=ALU.mult, op1=ALU.mult)
                last.then_inc(a_made, 1)
                dve.wait_ge(a_made, h * 4 + 2 * d + 1)
                dve.tensor_tensor(Tm[d][:, :, :], amat[d][:, :, :], every(M_LVL + d), ALU.mult).then_inc(t_first, 1)
                dve.wait_ge(t_first, h * 2 + d + 1)
                dve.tensor_tensor(Tm[d][:, :, :], every(M_IDENT), Tm[d][:, :, :], ALU.subtract).then_inc(t_made, 1)
                dve.tensor_tensor(aT[d][:, :, :], chunked(bank[1][:, :]), aT[d][:, :, :], ALU.mult)
                dve.tensor_tensor(qd[d][:, :, :], chunked(qn[:, :]), qd[d][:, :, :], ALU.mult).then_inc(a_made, 1)
            for lvl in range(1, LEVELS):
                m = lvl - 1
                for d in range(2):
                    dve.wait_ge(y_mm[d], h * 6 + m + 1)
                    dve.tensor_tensor(Ym[d][:, :, :], chunked(bank[2 + d][:, :]), every(M_LVL + 2 * lvl + 1 - d), ALU.mult).then_inc(y_masked[d], 1)
                for d in range(2):
                    dve.wait_ge(xp_mm[d], h * 6 + m + 1)
                    if lvl == 1:
                        dve.wait_ge(x_copied, h * 2 + d + 1)
                    else:
                        dve.wait_ge(x_upd[d], h * 6 + m)
                    dve.tensor_tensor(Xm[d][:, :, :], Xm[d][:, :, :], chunked(bank[d][:, :]), ALU.subtract).then_inc(x_upd[d], 1)
                    if lvl < LEVELS - 1:
                        dve.wait_ge(tp_mm[d], h * 5 + m + 1)
                        if lvl == 1:
                            dve.wait_ge(t_made, h * 2 + d + 1)
                        else:
                            dve.wait_ge(t_upd[d], h * 5 + m)
                        dve.tensor_tensor(Tm[d][:, :, :], Tm[d][:, :, :], chunked(bank[2 + d][:, :]), ALU.subtract).then_inc(t_upd[d], 1)
            dve.wait_ge(bv_done, h + 1)
            for s in range(NCH):
                for d in range(2):
                    c = s if d == 0 else NCH - 1 - s
                    if s:
                        dve.wait_ge(ks_mm[d], h * 3 + s)
                        dve.scalar_tensor_tensor(out=resid[d][:, :], in0=bank[4 + d][:, 0:P], scalar=hs[:, d, SC_NBE, c:c + 1], in1=bv[d][:, c, :], op0=ALU.mult, op1=ALU.add).then_inc(resid_done[d], 1)
                for d in range(2):
                    c = s if d == 0 else NCH - 1 - s
                    if s < NCH - 1:
                        dve.wait_ge(kv_mm[d], h * 3 + s + 1)
                        kv = bank[4 + d][:, 2 * P:3 * P]
                        if s == 0:
                            dve.tensor_copy(state[d][:, :], kv).then_inc(state_upd[d], 1)
                        else:
                            dve.wait_ge(state_upd[d], h * 3 + s)
                            dve.scalar_tensor_tensor(out=state[d][:, :], in0=state[d][:, :], scalar=hs[:, d, SC_EGL, c:c + 1], in1=kv, op0=ALU.mult, op1=ALU.add).then_inc(state_upd[d], 1)
            dve.wait_ge(of_copied, h + 1)
            dve.tensor_tensor(o_t[:, :], bank[7][:, :], o_t[:, :], ALU.add).then_inc(o_sum, 1)
            dve.wait_ge(o_rinv, h + 1)
            dve.wait_ge(o_sum, h + 1)
            dve.scalar_tensor_tensor(out=o_t[:, :], in0=o_t[:, :], scalar=par[:, ONW:ONW + 1], in1=nsq[1][:, :], op0=ALU.mult, op1=ALU.mult).then_inc(o_normed, 1)
            dve.wait_ge(o_normed, h + 1)
            dve.wait_ge(z_in, h * 16 + 16)
            dve.wait_ge(y_stored, h * 16)
            dve.tensor_tensor(y_t[:, :], o_t[:, :], z_s[:, :], ALU.mult).then_inc(y_gated, 1)

        def restage_lo(hi, lo, base):
            for k in range(KT):
                dve.wait_ge(re_hi, base + k + 1)
                dve.tensor_tensor(lo[:, k, :], restg[k % 4][:, :], hi[:, k, :].bitcast(FP32), ALU.subtract).then_inc(re_lo, 1)

        restage_lo(y_hi, y_lo, 0)
        with dve.Fori(0, MERGE_BLOCKS) as i:
            for g, buf in enumerate((gA, gB)):
                for j in range(2):
                    split_lo(i * 6 + (S_MERGE + 2 + 2 * g + j), j)
                    ada_beside(i + (ADA_A + ADA_P1), 2 * g + j)
                dve.wait_ge(gate_exp[g], i + 1)
                dve.tensor_scalar(buf[:, :, :], buf[:, :, :], 1.0, None, ALU.add).then_inc(gate_step, 1)
                dve.wait_ge(gate_step, i * 2 + g + 1)
                dve.reciprocal(buf[:, :, :], buf[:, :, :]).then_inc(gates_done, 1)
            ada_finish(i + (ADA_A + ADA_P1), bank[6][:, 0:4])
            split_lo(i * 6 + (S_MERGE + 6), 0)
            dve.wait_ge(gates_done, i * 2 + 2)
            dve.wait_ge(slot_used, i * 6 + (S_MERGE + 5))
            for t in range(2):
                last = dve.tensor_tensor(gA[:, t, :], bank[4 + t][:, :], gA[:, t, :], ALU.mult)
            last.then_inc(dn_merged, 1)
            split_lo(i * 6 + (S_MERGE + 7), 1)
            dve.wait_ge(slot_used, i * 6 + (S_MERGE + 6))
            for t in range(2):
                last = dve.tensor_tensor(gB[:, t, :], bank[6 + t][:, :], gB[:, t, :], ALU.mult)
            last.then_inc(sw_merged, 1)
            dve.wait_ge(dn_merged, i + 1)
            dve.wait_ge(sw_merged, i + 1)
            dve.tensor_tensor(gA[:, :, :], gA[:, :, :], gB[:, :, :], ALU.add).then_inc(mg_full, 1)

        dve.wait_ge(mod_done, ADA_ALL)
        restage_lo(act_hi, act_lo, KT)
        dve.wait_ge(x_back, 16)
        with dve.Fori(0, OUT_BODIES) as i:
            for b in range(2):
                for j in range(2):
                    split_lo(i * 4 + (S_OUT + 2 + 2 * b + j), j)
                dve.wait_ge(slot_used, i * 4 + (S_OUT + 2 * b + 2))
                for t in range(2):
                    k = i * 4 + (2 * b + t)
                    tile = xs[:, bass.ds(k, 1), :].rearrange("p a n -> p (a n)")
                    last = dve.scalar_tensor_tensor(out=tile, in0=bank[2 * b + t][:, :], scalar=mod[:, bass.ds(k + GA1, 1)], in1=tile, op0=ALU.mult, op1=ALU.add)
                last.then_inc(x1_done[b], 1)
        for b in range(2):
            dve.wait_ge(x1_done[b], OUT_BODIES)
        norm(1)

        def mlp_in(c):
            with dve.Fori(0, 2) as i:
                for b in range(2):
                    split_lo(c * 16 + i * 4 + (S_MLP + 2 + 2 * b), 0)
                    dve.wait_ge(u_relu[b], c * 2 + i + 1)
                    dve.tensor_tensor(urelu[b][:, :, :], urelu[b][:, :, :], urelu[b][:, :, :], ALU.mult).then_inc(u_sq[b], 1)
                    dve.wait_ge(u_sq[b], c * 2 + i + 1)
                    dve.wait_ge(u_high[b], c * 2 + i + 1)
                    dve.tensor_tensor(u_lo[:, bass.ds(i * 4 + 2 * b, 2), :], urelu[b][:, :, :], u_hi[:, bass.ds(i * 4 + 2 * b, 2), :].bitcast(FP32), ALU.subtract).then_inc(u_ready[b], 1)
                    split_lo(c * 16 + i * 4 + (S_MLP + 3 + 2 * b), 1)

        def mlp_out(c, i, j, split=True):
            if split:
                split_lo(c * 16 + i * 4 + (S_MLP + 10 + j), j % 2)
            dve.wait_ge(slot_used, c * 16 + i * 4 + (S_MLP + 9 + j))
            for q in range(4):
                dve.wait_ge(y_added[q], c * 2 + i) if q == j else None
            for t in range(2):
                k = i * 8 + (2 * j + t)
                tile = xs[:, bass.ds(k, 1), :].rearrange("p a n -> p (a n)")
                last = dve.scalar_tensor_tensor(out=tile, in0=bank[2 * j + t][:, :], scalar=mod[:, bass.ds(k + GA2, 1)], in1=tile, op0=ALU.mult, op1=ALU.add)
            last.then_inc(y_added[j], 1)

        with dve.Fori(0, CHUNKS - 1) as c:
            mlp_in(c)
            with dve.Fori(0, 2) as i:
                for j in range(4):
                    mlp_out(c, i, j)
        mlp_in(CHUNKS - 1)
        for i in range(2):
            for j in range(4):
                mlp_out(CHUNKS - 1, i, j, split=4 * i + j < 6)

    @block.tensor
    def _(pe):
        def slot(s, b, banks, hi, lo, k0, first, last, ready=None):
            pe.wait_ge(lo_done, s + 1)
            for k in range(ROWS):
                if ready:
                    ready(k)
                for t in range(2):
                    w = slice(k * COLS + t * P, k * COLS + (t + 1) * P)
                    pe.matmul(banks[t][:, :], w_hi[b][:, w], hi[:, k0 + k, :], start=first and k == 0, stop=False)
                    pe.matmul(banks[t][:, :], w_hi[b][:, w], lo[:, k0 + k, :], start=False, stop=False)
                    end = pe.matmul(banks[t][:, :], w_lo[b][:, w], hi[:, k0 + k, :], start=False, stop=last and k == ROWS - 1)
            end.then_inc(slot_used, 1)

        def ada_sum(g, b):
            pe.wait_ge(ada_step, g * 16 + 16)
            for j in range(4):
                last = pe.matmul(b[:, j:j + 1], ada_acc[:, j * P:(j + 1) * P], ones[:, 0:1], start=True, stop=True)
            last.then_inc(ada_summed, 1)

        def residual_sum(n):
            for k in range(KT):
                pe.wait_ge(sq_done, KT * n + k + 1)
                mm = pe.matmul(bank[0][:, :], ones[:, :], sq[k % 2][:, :], start=k == 0, stop=k == KT - 1)
                mm.then_inc(sq_used, 1)

        pe.wait_ge(ones_set, 1)
        residual_sum(0)
        with pe.Fori(0, ADA_A) as g:
            pe.wait_ge(mod_done, g)
            ada_sum(g, bank[7])

        pe.wait_ge(h_lo, KT)
        pe.wait_ge(h_hi, KT)

        def projections(first, n, with_ada):
            with pe.Fori(0, n) as i:
                for b in range(2):
                    pe.wait_ge(evac[b], i + first)
                    for j in range(2):
                        slot(i * 4 + (4 * first + 2 * b + j), j, bank[2 * b:2 * b + 2], act_hi, act_lo, ROWS * j, j == 0, j == 1)
                if with_ada:
                    pe.wait_ge(mod_done, i + ADA_A)
                    ada_sum(i + ADA_A, bank[7])

        projections(0, SW_BODIES, False)
        projections(SW_BODIES, DN_BODIES + Z_BODIES, True)

        pe.wait_ge(sp_lo_done, 1)
        for c in range(NCH):
            out = bank[4][:, 32 * c:32 * c + 32]
            for k in range(KT):
                tok = slice(c * P, (c + 1) * P)
                w = slice(32 * k, 32 * k + 32)
                pe.matmul(out, act_hi[:, k, tok], sp_hi[:, w], start=k == 0, stop=False)
                pe.matmul(out, act_lo[:, k, tok], sp_hi[:, w], start=False, stop=False)
                last = pe.matmul(out, act_hi[:, k, tok], sp_lo[:, w], start=False, stop=k == KT - 1)
        last.then_inc(sp_summed, 1)
        pe.wait_ge(sp_dve, SP_G)
        for n, m in enumerate((tri[:, 0, :], tri[:, 1, :], ones[:, :])):
            last = pe.matmul(bank[5][:, 64 * n:64 * n + 64], m, g_tok[:, :, :].rearrange("p c n -> p (c n)"), start=True, stop=True)
        last.then_inc(cums_done, 1)

        def rotate(n, q):
            pe.wait_ge(aq_sq, n + 1)
            pe.matmul(bank[0][:, :], ones[:, :], q_sq[:, :], start=True, stop=True).then_inc(aq_summed, 1)
            pe.wait_ge(aq_normed, n + 1)
            pe.matmul(bank[1][:, :], rot_m, q[:, :], start=True, stop=True).then_inc(aq_turned, 1)

        pe.wait_ge(mask_in, 32)
        pe.wait_ge(kv_in, 32 * KV_HEADS)
        for n in range(KV_HEADS):
            for c in range(NCH):
                last = pe.transpose(bank[2 + n][:, c * P:(c + 1) * P], v_raw[n][:, c * P:(c + 1) * P], a_id[:, :])
            last.then_inc(av_turned, 1)
            rotate(n, k_fin[n])
            pe.wait_ge(aq_roped, n + 1)
        pe.wait_ge(av_copied, KV_HEADS)
        for kv in range(KV_HEADS):
            with pe.Fori(0, 2) as i:
                for b in range(2):
                    h = i * 2 + (4 * kv + b)
                    pe.wait_ge(ao_copied, h)
                    rotate(h + KV_HEADS, q_nrm)
                    pe.wait_ge(aq_roped, h + KV_HEADS + 1)
                    for c in range(NCH):
                        lo, hi = max(c - 1, 0), min(c + 2, NCH)
                        last = pe.matmul(bank[4 + c][:, (lo - c + 1) * P:(hi - c + 1) * P], q_nrm[:, c * P:(c + 1) * P], k_fin[kv][:, lo * P:hi * P], start=True, stop=True)
                    last.then_inc(scores_mm, 1)
                    for c in range(NCH):
                        pe.wait_ge(p_ready, h * NCH + c + 1)
                        pe.wait_ge(p_copied[c % 2], h * 2 + c // 2)
                        for j in range(3):
                            last = pe.transpose(bank[2 + c % 2][:, j * P:(j + 1) * P], prob[:, c, j * P:(j + 1) * P], a_id[:, :])
                        last.then_inc(p_turned[c % 2], 1)
                    for c in range(NCH):
                        pe.wait_ge(p_copied[c % 2], h * 2 + c // 2 + 1)
                        keys = [j for j in range(3) if 0 <= c + j - 1 < NCH]
                        for j in keys:
                            last = pe.matmul(bank[1][:, c * P:(c + 1) * P], v_tok[kv][:, c + j - 1, :], prob_t[:, c, j * P:(j + 1) * P], start=j == keys[0], stop=j == keys[-1])
                    last.then_inc(ao_mm, 1)

        pe.wait_ge(dmask_in, 16)
        ident = dm[:, M_IDENT, :]

        def part(t, c):
            return t[:, c * P:(c + 1) * P]

        with pe.Fori(0, HEADS) as h:
            pe.wait_ge(head_in, h * 48 + 48)
            for c in range(NCH):
                last = pe.transpose(part(bank[3], c), qkv[:, 2, c * P:(c + 1) * P], ident)
            last.then_inc(v_turned, 1)
            for k in range(2):
                pe.wait_ge(qk_sq, h * 2 + k + 1)
                pe.matmul(bank[k][:, :], ones[:, :], nsq[k][:, :], start=True, stop=True).then_inc(qk_sum, 1)
            pe.wait_ge(qk_normed, h * 2 + 2)
            for c in range(NCH):
                last = pe.transpose(part(bank[2], c), part(kn, c), ident)
            last.then_inc(k_turned, 1)
            for c in range(NCH):
                pe.matmul(part(bank[0], c), part(kn, c), part(kn, c), start=True, stop=True)
            for c in range(NCH):
                last = pe.matmul(part(bank[1], c), part(kn, c), part(qn, c), start=True, stop=True)
            last.then_inc(grams, 1)
            pe.wait_ge(hs_set, h + 1)
            for d in (0, 1):
                pe.wait_ge(ktok_done, h + 1)
                for c in range(NCH):
                    last = pe.matmul(part(bank[2 + d], c), hs[:, d, SC_G, c:c + 1].to_broadcast([P, P]), dm[:, M_LE + d, :], start=True, stop=True)
                last.then_inc(gb_done, 1)
            for d in range(2):
                pe.wait_ge(t_made, h * 2 + d + 1)
                for c in range(NCH):
                    last = pe.transpose(part(bank[2 + d], c), Tm[d][:, c, :], ident)
                last.then_inc(x_turned, 1)
            for lvl in range(1, LEVELS):
                m = lvl - 1
                for d in range(2):
                    if lvl == 1:
                        pe.wait_ge(x_copied, h * 2 + d + 1)
                    else:
                        pe.wait_ge(x_upd[d], h * 6 + m)
                        pe.wait_ge(t_upd[d], h * 5 + m)
                    for c in range(NCH):
                        last = pe.matmul(part(bank[2 + d], c), amat[d][:, c, :], Xm[d][:, c, :], start=True, stop=True)
                    last.then_inc(y_mm[d], 1)
                if lvl == 1:
                    pe.wait_ge(a_made, h * 4 + 4)
                for d in range(2):
                    pe.wait_ge(y_masked[d], h * 6 + m + 1)
                    for c in range(NCH):
                        last = pe.matmul(part(bank[d], c), Tm[d][:, c, :], Ym[d][:, c, :], start=True, stop=True)
                    last.then_inc(xp_mm[d], 1)
                    if lvl < LEVELS - 1:
                        for c in range(NCH):
                            last = pe.matmul(part(bank[2 + d], c), Ym[d][:, c, :], Tm[d][:, c, :], start=True, stop=True)
                        last.then_inc(tp_mm[d], 1)
            for s in range(NCH):
                for d in range(2):
                    c = s if d == 0 else NCH - 1 - s
                    if s:
                        pe.wait_ge(state_upd[d], h * 3 + s)
                        pe.matmul(bank[4 + d][:, 0:P], part(kn, c), state[d][:, :], start=True, stop=True).then_inc(ks_mm[d], 1)
                for d in range(2):
                    c = s if d == 0 else NCH - 1 - s
                    if s:
                        pe.wait_ge(resid_done[d], h * 3 + s)
                        rhs = resid[d][:, :]
                    else:
                        pe.wait_ge(bv_done, h + 1)
                        pe.wait_ge(x_upd[d], h * 6 + 6)
                        rhs = bv[d][:, c, :]
                    pe.matmul(bank[4 + d][:, P:2 * P], Xm[d][:, c, :], rhs, start=True, stop=True).then_inc(vn_mm[d], 1)
                for d in range(2):
                    c = s if d == 0 else NCH - 1 - s
                    if s:
                        pe.matmul(part(bank[6 + d], c), state[d][:, :], qd[d][:, c, :], start=True, stop=False)
                    pe.wait_ge(v_copied[d], h * NCH + s + 1)
                    last = pe.matmul(part(bank[6 + d], c), vnew[d][:, :], aT[d][:, c, :], start=s == 0, stop=True)
                    if s < NCH - 1:
                        pe.matmul(bank[4 + d][:, 2 * P:3 * P], k_tok[:, c, :], vdec[d][:, :], start=True, stop=True).then_inc(kv_mm[d], 1)
            last.then_inc(o_mm, 1)
            pe.wait_ge(o_sq, h + 1)
            pe.matmul(bank[4][:, :], ones[:, :], nsq[0][:, :], start=True, stop=True).then_inc(o_summed, 1)

        pe.wait_ge(re_lo, KT)
        pe.wait_ge(o_rinv, HEADS)
        with pe.Fori(0, MERGE_BLOCKS) as i:
            for g in range(2):
                pe.wait_ge(gate_exp[g], i)
                for j in range(2):
                    slot(i * 6 + (S_MERGE + 2 * g + j), j, bank[2 * g:2 * g + 2], act_hi, act_lo, ROWS * j, j == 0, j == 1)
            pe.wait_ge(dn_merged, i)
            slot(i * 6 + (S_MERGE + 4), 0, bank[4:6], y_hi, y_lo, 0, True, True)
            pe.wait_ge(sw_merged, i)
            ada_sum(i + (ADA_A + ADA_P1), bank[6])
            pe.wait_ge(mod_done, i + (ADA_A + ADA_P1 + 1))
            slot(i * 6 + (S_MERGE + 5), 1, bank[6:8], y_hi, y_lo, ROWS, True, True)

        for g in range(2):
            pe.wait_ge(gate_exp[g], MERGE_BLOCKS)
        pe.wait_ge(re_lo, 2 * KT)
        with pe.Fori(0, OUT_BODIES) as i:
            for b in range(2):
                pe.wait_ge(x1_done[b], i)
                for j in range(2):
                    slot(i * 4 + (S_OUT + 2 * b + j), j, bank[2 * b:2 * b + 2], act_hi, act_lo, ROWS * j, j == 0, j == 1)
        for b in range(2):
            pe.wait_ge(x1_done[b], OUT_BODIES)
        residual_sum(1)

        pe.wait_ge(h_lo, 2 * KT)
        pe.wait_ge(h_hi, 2 * KT)
        with pe.Fori(0, CHUNKS) as c:
            with pe.Fori(0, 2) as i:
                for b in range(2):
                    pe.wait_ge(u_relu[b], c * 2 + i)
                    pe.wait_ge(y_added[b], c * 2)
                    for j in range(2):
                        slot(c * 16 + i * 4 + (S_MLP + 2 * b + j), j, bank[2 * b:2 * b + 2], act_hi, act_lo, ROWS * j, j == 0, j == 1)
            with pe.Fori(0, 2) as i:
                for j in range(4):
                    pe.wait_ge(y_added[j], c * 2 + i)
                    if j < 2:
                        pe.wait_ge(u_relu[j], c * 2 + 2)

                    def ready(k):
                        if j == 0 and k % 2 == 0:
                            pe.wait_ge(u_ready[(k // 2) % 2], c * 2 + (k // 4 + 1))

                    slot(c * 16 + i * 4 + (S_MLP + 8 + j), j % 2, bank[2 * j:2 * j + 2], u_hi, u_lo, 0, True, True, ready)

    ctx.close()


def _slots(w, k0, c0):
    part = w[k0:k0 + ROWS * P, c0:c0 + COLS]
    return part.reshape(ROWS, P, COLS).transpose(1, 0, 2).reshape(P, SLOT)


def _column(v):
    return np.asarray(v).reshape(-1, P).T


def _stream(w_in, w_dn, w_sw, w_out, w_mi, w_mo):
    small = 2 * D + 0
    out = np.empty((N_SLOTS, P, SLOT), np.float32)
    at = [0]

    def put(w, k0, c0):
        out[at[0]] = _slots(w, k0, c0)
        at[0] += 1

    def columns(w, c0, c1):
        for c in range(c0, c1, COLS):
            for k in range(0, w.shape[0], ROWS * P):
                put(w, k, c)

    sw = small + 4 * HEADS
    gates = sw + (HEADS + 2 * KV_HEADS) * P
    columns(w_in, sw, gates)
    columns(w_in, 0, small)
    for j in range(MERGE_BLOCKS):
        for w, c in ((w_in, gates + j * COLS), (w_in, gates + D + j * COLS), (w_dn, j * COLS), (w_sw, j * COLS)):
            columns(w, c, c + COLS)
    columns(w_out, 0, D)
    for c in range(CHUNKS):
        columns(w_mi, c * ROWS * P, (c + 1) * ROWS * P)
        columns(w_mo[c * ROWS * P:(c + 1) * ROWS * P], 0, D)
    assert at[0] == N_SLOTS
    return out


def kernel(x, c, w_ada, b_ada, norm1_w, w_in, conv_w, dn_a_log, dn_dt_bias, dn_out_norm_w,
           w_dn_proj, q_norm_w, k_norm_w, sink, w_swa_proj, w_out, norm2_w, w_mlp_in, w_mlp_out):
    import concourse.bacc as bacc
    from concourse.bass_utils import run_bass_kernel_spmd

    def row(v, n):
        return np.broadcast_to(np.asarray(v, np.float32).reshape(1, n), (P, n))

    w_in = np.asarray(w_in)[0]
    params = np.concatenate([
        _column(c), _column(b_ada), _column(norm1_w), _column(norm2_w),
        np.asarray(conv_w)[0].reshape(CONV_K, QKV_T, P).transpose(2, 1, 0).reshape(P, QKV_T * CONV_K),
        _column(dn_out_norm_w), _column(q_norm_w), _column(k_norm_w),
        row(dn_dt_bias, 16), row(dn_a_log, 16), row(sink, HEADS),
        row([EPS, math.log(SCALE), 1.0], 3)], axis=1)
    arrays = {
        "wstream": _stream(w_in, *(np.asarray(w)[0] for w in (w_dn_proj, w_swa_proj, w_out, w_mlp_in, w_mlp_out))),
        "adastream": np.asarray(w_ada)[0].reshape(4, 4, P, ADA_G, 512).transpose(3, 0, 2, 1, 4).reshape(4 * ADA_G, P, SLOT),
        "wsmall": w_in[:, 2 * D:2 * D + 32].reshape(KT, P, 32).transpose(1, 0, 2).reshape(P, KT * 32),
        "xT": np.asarray(x)[0].T,
        "params": params,
        "maskc": masks(),
    }
    arrays = {f"in_{n}_dram": np.ascontiguousarray(a) for n, a in arrays.items()}
    nc = bacc.Bacc("TRN2", target_bir_lowering=False, num_devices=1)
    args = [nc.dram_tensor(n, a.shape, mybir.dt.from_np(a.dtype), kind="ExternalInput").ap() for n, a in arrays.items()]
    args.append(nc.dram_tensor("out_0_dram", (D, SEQ), FP32, kind="ExternalOutput").ap())
    hybrid_block_kernel(nc, *args)
    r = run_bass_kernel_spmd(nc, [arrays], core_ids=[0])
    return np.ascontiguousarray(r.results[0]["out_0_dram"].T)[None]
```

```python
import math
from contextlib import ExitStack

import concourse.bass as bass
from concourse import mybir
import numpy as np

FP32 = mybir.dt.float32
FP32R = mybir.dt.float32r
ACT = mybir.ActivationFunctionType
ALU = mybir.AluOpType
AX = mybir.AxisListType

P = 128
SEQ, D, DFF = 512, 2048, 8192
KT = D // P
HEADS, KV_HEADS = 8, 2
NCH = SEQ // P
CONV_K = 5
EPS = 1e-6
SCALE = float(P) ** -0.5
QKV_T, Z_T = 24, 8
LEVELS = 7

ROWS, COLS = 8, 256
SLOT = ROWS * COLS
SW_BODIES, DN_BODIES, Z_BODIES, OUT_BODIES = 3, 6, 2, 4
BLOCKS = D // COLS
CHUNKS = DFF // (ROWS * P)
S_ATT = 4 * (SW_BODIES + DN_BODIES + Z_BODIES)
S_DELTA = S_ATT + 2 * HEADS
S_MERGE = S_DELTA + 2 * HEADS
S_OUT = S_MERGE + 2 * BLOCKS
S_MLP = S_OUT + 4 * OUT_BODIES
N_SLOTS = S_MLP + 16 * CHUNKS
ADA_G = 6 * D // 512
ADA_A = 8
ADA_DN = ADA_A + 2 * SW_BODIES
ADA_Z = ADA_DN + DN_BODIES

C_COL, BADA, N1W, N2W, CONVW = 0, 16, 112, 128, 144
ONW, QNW, KNW, DTB, ALOG, SINK, EPSC, LNS, ONEC = 264, 265, 266, 267, 283, 299, 307, 308, 309
N_PAR = 310
SH1, SC1, GA1, SH2, SC2, GA2 = (KT * n for n in range(6))

M_IDENT, M_LE, M_GE = 0, 1, 2
M_KEEP_T, M_KEEP = 3, 5
M_LVL = 7
M_BAND, M_ROT, M_COS, M_SIN = 21, 24, 25, 29
N_MASK = 33


def masks():
    i = np.arange(P)
    r, c = i[:, None], i[None, :]
    huge = np.float32(1e30)
    m = [r == c, r <= c, r >= c]
    m += [np.where(r <= c, 0, -huge), np.where(r >= c, 0, -huge)]
    m += [np.where(r > c, 0, huge), np.where(r < c, 0, huge)]
    for lvl in range(LEVELS):
        b = 1 << lvl
        low = ((r // b) % 2 == 1) & (c // b == r // b - 1)
        m += [low, low.T]
    m += [np.where(c >= r, 0, -huge), np.zeros((P, P)), np.where(c <= r, 0, -huge)]
    rot = np.zeros((P, P))
    half = P // 8
    for k in range(half):
        rot[half + k, k] = -1.0
        rot[k, half + k] = 1.0
    m.append(rot)
    inv = (np.float32(500000.0) ** (-np.arange(half, dtype=np.float32) * np.float32(2.0) / np.float32(2 * half))).astype(np.float32)
    ang = (np.arange(SEQ, dtype=np.float32)[:, None] * inv[None, :]).astype(np.float32)
    cos, sin = np.zeros((P, SEQ)), np.zeros((P, SEQ))
    cos[:half] = cos[half:2 * half] = np.cos(ang).T
    sin[:half] = sin[half:2 * half] = np.sin(ang).T
    m += [cos, sin]
    return np.ascontiguousarray(np.concatenate([np.asarray(x, np.float32) for x in m], axis=1))


SC_G, SC_GC, SC_BETA, SC_NBE, SC_KD, SC_EGL = range(6)
SP_G, SP_LEFT, SP_DVE_ALL, SP_ACT_ALL = 6, 7, 20, 11


def hybrid_block_kernel(nc, wstream, adastream, wsmall, xT, params, maskc, outT):
    ctx = ExitStack()
    cursor = [16512]

    def size_of(shape):
        return (4 * int(np.prod(shape[1:])) + 31) // 32 * 32

    def lasting(name, shape, dt=FP32):
        t = nc.alloc_sbuf_tensor_at(name, shape, dt, offset=cursor[0])
        cursor[0] += size_of(shape)
        return t

    raw = [lasting(f"raw{b}", [P, SLOT]) for b in range(4)]
    w_hi = [lasting(f"w_hi{b}", [P, SLOT], FP32R) for b in range(2)]
    w_lo = [lasting(f"w_lo{b}", [P, SLOT], FP32R) for b in range(2)]
    act_hi = lasting("act_hi", [P, KT, SEQ], FP32R)
    act_lo = lasting("act_lo", [P, KT, SEQ], FP32R)
    par = lasting("par", [P, N_PAR])
    ones = lasting("ones", [P, P])
    csilu = lasting("csilu", [P, KT])
    mod = lasting("mod", [P, 6 * KT])
    gain = lasting("gain", [P, 2, KT])
    ada_acc = [lasting(f"ada_acc{b}", [P, 512]) for b in range(2)]
    scal = lasting("scal", [P, HEADS, 2, 6, NCH])
    phase_base = cursor[0]
    raw_at = 16512
    gst = [nc.alloc_sbuf_tensor_at(f"gst{b}", [P, 2, SEQ], FP32, offset=raw_at + 4 * SLOT * 2 + b * 4 * 2 * SEQ) for b in range(2)]
    gates = [nc.alloc_sbuf_tensor_at(f"gates{b}", [P, 4, SEQ], FP32, offset=raw_at + 4 * SLOT * (2 + b)) for b in range(2)]

    def phase(start=0):
        where = [phase_base + start]

        def take(name, shape, dt=FP32):
            t = nc.alloc_sbuf_tensor_at(name, shape, dt, offset=where[0])
            where[0] += size_of(shape)
            return t

        return take

    r = phase()
    xs = r("xs", [P, KT, SEQ])
    sq = [r(f"sq{b}", [P, 2, SEQ]) for b in range(2)]
    rstd = r("rstd", [P, SEQ])
    lnb = r("lnb", [P, SEQ])
    scaled = [r(f"scaled{b}", [P, SEQ]) for b in range(4)]
    r = phase()
    xpad = [r(f"xpad{b}", [P, 2, SEQ + CONV_K - 1]) for b in range(2)]
    stg = [r(f"stg{b}", [P, 2, SEQ]) for b in range(2)]
    sp_raw = r("sp_raw", [P, KT * 32])
    sp_hi = r("sp_hi", [P, KT * 32], FP32R)
    sp_lo = r("sp_lo", [P, KT * 32], FP32R)
    tri = r("tri", [P, 2, P])
    logits = r("logits", [P, NCH, 32])
    (e_beta, a_raw, a_abs, a_exp, a_ln, a_soft, g_tok, g_cum, g_sum, g_left, e_cum, e_left, e_sum, nbe) = (
        r(f"s_{n}", [P, NCH, 16]) for n in range(14))
    e_alog = r("e_alog", [P, 16])
    r = phase()
    am = r("am", [P, 12, P])
    a_id = r("a_id", [P, P])
    k_fin = [r(f"k_fin{n}", [P, SEQ]) for n in range(KV_HEADS)]
    v_tok = [r(f"v_tok{n}", [P, NCH, P]) for n in range(KV_HEADS)]
    q_raw = [r(f"q_raw{b}", [P, SEQ]) for b in range(2)]
    v_raw = [r(f"v_raw{b}", [P, SEQ]) for b in range(2)]
    q_sq = r("q_sq", [P, SEQ])
    q_ri = r("q_ri", [P, SEQ])
    q_nrm = r("q_nrm", [P, SEQ])
    rtmp = r("rtmp", [P, SEQ])
    prob = r("prob", [P, NCH, 3 * P])
    prob_t = r("prob_t", [P, NCH, 3 * P])
    s_max, s_neg, s_sum, s_sink, e_sink, s_inv = (r(f"a_{n}", [P, NCH]) for n in range(6))
    a_out = [r(f"a_out{b}", [P, SEQ]) for b in range(2)]
    band, rot_m = am[:, 0:3, :], am[:, 3, :]
    cos_t = am[:, 4:8, :].rearrange("p a n -> p (a n)")
    sin_t = am[:, 8:12, :].rearrange("p a n -> p (a n)")
    r = phase()
    dm = r("dm", [P, M_BAND, P])
    qkv = r("qkv", [P, 3, SEQ])
    z_s = r("z_s", [P, SEQ])
    hs = r("hs", [P, 2, 6, NCH])
    qn = r("qn", [P, SEQ])
    kn = r("kn", [P, SEQ])
    nsq = [r(f"nsq{n}", [P, SEQ]) for n in range(2)]
    k_tok = r("k_tok", [P, NCH, P])
    bv, aT, amat, qd, Tm, Xm, Ym = ([r(f"{n}{d}", [P, NCH, P]) for d in range(2)] for n in ("bv", "aT", "amat", "qd", "Tm", "Xm", "Ym"))
    state, resid, vnew, vdec = ([r(f"{n}{d}", [P, P]) for d in range(2)] for n in ("state", "resid", "vnew", "vdec"))
    o_t = r("o_t", [P, SEQ])
    y_t = r("y_t", [P, SEQ])
    r = phase()
    y_hi = r("y_hi", [P, KT, SEQ], FP32R)
    y_lo = r("y_lo", [P, KT, SEQ], FP32R)
    r = phase(2 * KT * SEQ * 4)
    restg = [r(f"restg{b}", [P, SEQ]) for b in range(4)]
    r = phase(KT * SEQ * 4)
    u_hi = r("u_hi", [P, ROWS, SEQ], FP32R)
    u_lo = r("u_lo", [P, ROWS, SEQ], FP32R)
    urelu = [r(f"urelu{b}", [P, 2, SEQ]) for b in range(2)]

    bank = [ctx.enter_context(nc.psum_tensor(f"bank{n}", [P, 512], FP32)) for n in range(8)]

    def chunked(ap, n=NCH):
        return ap.rearrange("p (c n) -> p c n", c=n)

    def scratch(name, n):
        return nc.dram_tensor(name, [n, P, SEQ], FP32)

    sw_d, dn_d, z_d = scratch("sw_d", 12), scratch("dn_d", QKV_T), scratch("z_d", Z_T)
    y_d, gate_d = scratch("y_d", KT), scratch("gate_d", 2 * KT)

    def tiles_of(t, first, n=1):
        return t[bass.ds(first, n)].rearrange("a p n -> p a n")

    def sem(name):
        return ctx.enter_context(nc.semaphore(name))

    def sems(name, n=2):
        return [sem(f"{name}{b}") for b in range(n)]

    raw_full = sems("raw_full", 4)
    par_in, x_in, x_back, mask_in, sp_in, kv_in = (sem(n) for n in ("par_in", "x_in", "x_back", "mask_in", "sp_in", "kv_in"))
    stg_stored, q_in, a_stored, gst_stored = sems("stg_stored"), sems("q_in"), sems("a_stored"), sems("gst_stored")
    head_in, z_in, y_stored = sem("head_in"), sem("z_in"), sem("y_stored")
    restg_in, gates_in, out_stored = sems("restg_in", 4), sems("gates_in"), sem("out_stored")
    stg_free, a_free, gst_free, y_free = (sem(n) for n in ("stg_free", "a_free", "gst_free", "y_free"))
    hi_done, lo_done, slot_used = sem("hi_done"), sem("lo_done"), sem("slot_used")
    c_silu = sem("c_silu")
    ada_step, ada_summed, mod_done = sem("ada_step"), sem("ada_summed"), sem("mod_done")
    ones_set, pad_set = sem("ones_set"), sem("pad_set")
    sq_done, sq_used, ln_done, rstd_done = (sem(n) for n in ("sq_done", "sq_used", "ln_done", "rstd_done"))
    gain_done, scaled_done, h_hi, h_lo = (sem(n) for n in ("gain_done", "scaled_done", "h_hi", "h_lo"))
    evac, silu_done, conv_step, gate_out = sems("evac"), sem("silu_done"), sem("conv_step"), sem("gate_out")
    sp_hi_done, sp_lo_done, sp_summed, cums_done, sp_act, sp_dve = (sem(n) for n in ("sp_hi_done", "sp_lo_done", "sp_summed", "cums_done", "sp_act", "sp_dve"))
    aq_sq, aq_summed, aq_ln, aq_rinv, aq_normed, aq_turned, aq_roped, aq_step = (
        sem(n) for n in ("aq_sq", "aq_summed", "aq_ln", "aq_rinv", "aq_normed", "aq_turned", "aq_roped", "aq_step"))
    av_turned, av_copied = sem("av_turned"), sem("av_copied")
    scores_mm, scored, maxed, negated, p_exp, sink_exp, p_step, p_ready = (
        sem(n) for n in ("scores_mm", "scored", "maxed", "negated", "p_exp", "sink_exp", "p_step", "p_ready"))
    p_turned, p_copied, ao_mm, ao_copied = sem("p_turned"), sems("p_copied"), sem("ao_mm"), sem("ao_copied")
    qk_sq, qk_sum, qk_ln, qk_rinv, qk_normed, hs_set = (sem(n) for n in ("qk_sq", "qk_sum", "qk_ln", "qk_rinv", "qk_normed", "hs_set"))
    v_turned, bv_done, k_turned, ktok_done, grams, gb_done = (sem(n) for n in ("v_turned", "bv_done", "k_turned", "ktok_done", "grams", "gb_done"))
    exponents, decays, a_made, t_first, t_made, x_turned, x_copied = (
        sem(n) for n in ("exponents", "decays", "a_made", "t_first", "t_made", "x_turned", "x_copied"))
    y_mm, y_masked, xp_mm, tp_mm, x_upd, t_upd = (sems(n) for n in ("y_mm", "y_masked", "xp_mm", "tp_mm", "x_upd", "t_upd"))
    ks_mm, resid_done, vn_mm, v_copied, kv_mm, state_upd = (sems(n) for n in ("ks_mm", "resid_done", "vn_mm", "v_copied", "kv_mm", "state_upd"))
    o_mm, of_copied, o_sum, o_sq, o_summed, o_ln, o_rinv, o_normed, y_gated = (
        sem(n) for n in ("o_mm", "of_copied", "o_sum", "o_sq", "o_summed", "o_ln", "o_rinv", "o_normed", "y_gated"))
    re_hi, re_lo = sem("re_hi"), sem("re_lo")
    gates_open, merged, m_full, m_hi, m_lo = sem("gates_open"), sems("merged"), sem("m_full"), sem("m_hi"), sem("m_lo")
    x1_done = sem("x1_done")
    u_relu, u_sq, u_high, u_ready, y_added = sems("u_relu"), sem("u_sq"), sem("u_high"), sems("u_ready"), sems("y_added", 4)

    block = ctx.enter_context(nc.Block())
    Y_ORDER = [*range(HEADS, KT), *range(HEADS)]
    GATE_HEADS = BLOCKS

    @block.sync
    def _(sp):
        sp.dma_start(par[:, :], params).then_inc(par_in, 16)
        sp.dma_start(xs[:, :, :], xT.rearrange("(k p) n -> p k n", p=P)).then_inc(x_in, 16)

        def load(stream, s, b):
            sp.dma_start(raw[b][:, :], stream[bass.ds(s, 1)].rearrange("a p n -> (a p) n")).then_inc(raw_full[b], 16)

        for j in range(4):
            load(adastream, j, j)
        with sp.Fori(1, ADA_A) as g:
            for j in range(4):
                sp.wait_ge(ada_step, g * 16 + 4 * j - 12)
                load(adastream, g * 4 + j, j)
        for j in range(2):
            sp.wait_ge(ada_step, 16 * ADA_A - 12 + 4 * j)
            load(wstream, j, j)

        def load_w(s, b):
            sp.wait_ge(lo_done, s - 1)
            load(wstream, s, b)

        def load_ada(g, j):
            sp.wait_ge(ada_step, g * 16 + 4 * j - 4)
            load(adastream, g * 4 + j, 2 + j % 2)

        def load_body(i, first, g, groups):
            for j in range(4):
                load_w(i * 4 + (4 * first + 2 + j), j % 2)
                for q in range(groups * j, groups * (j + 1)):
                    load_ada(g + q // 4, q % 4)

        with sp.Fori(0, SW_BODIES) as i:
            load_body(i, 0, i * 2 + ADA_A, 2)
        with sp.Fori(0, DN_BODIES) as i:
            load_body(i, SW_BODIES, i + ADA_DN, 1)
        with sp.Fori(0, Z_BODIES) as i:
            load_body(i, SW_BODIES + DN_BODIES, i * 2 + ADA_Z, 2)
        with sp.Fori(0, (N_SLOTS - S_ATT - 2) // 2) as i:
            for j in range(2):
                load_w(i * 2 + S_ATT + 2 + j, j)
        sp.wait_ge(out_stored, 16 * BLOCKS)

    @block.gpsimd
    def _(pool):
        for free, buffers in ((stg_free, 2), (a_free, 2), (gst_free, 2), (y_free, 1)):
            pool.sem_inc(free, buffers)
        pool.memset(ones[:, :], 1.0).then_inc(ones_set, 1)
        pool.wait_ge(h_hi, KT)
        pool.wait_ge(h_lo, KT)
        for b in range(2):
            pool.memset(xpad[b][:, :, :], 0.0).then_inc(pad_set, 1)
        pool.dma_start(sp_raw[:, :], wsmall).then_inc(sp_in, 16)
        pool.dma_start(tri[:, :, :], chunked(maskc[:, P * M_LE:P * (M_GE + 1)], 2)).then_inc(sp_in, 16)

        def store_block(dst, i, n, b):
            pool.dma_start(tiles_of(dst, i * 4 + 2 * b, 2), stg[b][:, :, :]).then_inc(stg_stored[b], 16)
            pool.wait_ge(stg_stored[b], (i + n + 1) * 16)
            pool.sem_inc(stg_free, 1)

        with pool.Fori(0, SW_BODIES) as i:
            for b in range(2):
                pool.wait_ge(evac[b], i + 2)
                store_block(sw_d, i, 0, b)
        with pool.Fori(0, DN_BODIES) as i:
            for b in range(2):
                pool.wait_ge(silu_done, i * 2 + b + 1)
                store_block(dn_d, i, SW_BODIES, b)
        with pool.Fori(0, Z_BODIES) as i:
            for b in range(2):
                pool.wait_ge(evac[b], i + (SW_BODIES + DN_BODIES + 2))
                store_block(z_d, i, SW_BODIES + DN_BODIES, b)

        pool.wait_ge(sp_dve, SP_DVE_ALL)
        pool.wait_ge(sp_act, SP_ACT_ALL)
        pool.dma_start(am[:, :, :], chunked(maskc[:, P * M_BAND:], 12)).then_inc(mask_in, 16)
        pool.dma_start(a_id[:, :], maskc[:, 0:P]).then_inc(mask_in, 16)
        for n in range(KV_HEADS):
            pool.dma_start(q_raw[n][:, :], sw_d[HEADS + n]).then_inc(kv_in, 16)
            pool.dma_start(v_raw[n][:, :], sw_d[HEADS + KV_HEADS + n]).then_inc(kv_in, 16)
        for b in range(2):
            pool.wait_ge(aq_normed, b + 1)
            pool.dma_start(q_raw[b][:, :], sw_d[b]).then_inc(q_in[b], 16)

        def store_gates(n, b, before):
            pool.wait_ge(gate_out, n + 2)
            pool.dma_start(tiles_of(gate_d, n * 2, 2), gst[b][:, :, :]).then_inc(gst_stored[b], 16)
            pool.wait_ge(gst_stored[b], (before + 1) * 16)
            pool.sem_inc(gst_free, 1)

        def store_head(i, b):
            store_gates(i * 2 + b, b, i)
            pool.wait_ge(ao_copied, i * 2 + (b + 2))
            pool.dma_start(tiles_of(y_d, i * 2 + (HEADS + b)), a_out[b][:, :].unsqueeze(1)).then_inc(a_stored[b], 16)
            pool.wait_ge(a_stored[b], (i + 1) * 16)
            pool.sem_inc(a_free, 1)

        with pool.Fori(0, HEADS // 2 - 1) as i:
            for b in range(2):
                pool.wait_ge(aq_normed, i * 2 + KV_HEADS + b + 1)
                pool.dma_start(q_raw[b][:, :].unsqueeze(1), tiles_of(sw_d, i * 2 + 2 + b)).then_inc(q_in[b], 16)
                store_head(i, b)
        for b in range(2):
            store_head(HEADS // 2 - 1, b)

        pool.dma_start(dm[:, :, :], chunked(maskc[:, 0:P * M_BAND], M_BAND)).then_inc(mask_in, 16)

        def load_head(h):
            for n in range(3):
                pool.dma_start(qkv[:, n:n + 1, :], tiles_of(dn_d, h + HEADS * n)).then_inc(head_in, 16)

        load_head(0)
        pool.dma_start(z_s[:, :], z_d[0]).then_inc(z_in, 16)
        with pool.Fori(0, HEADS - 1) as h:
            pool.wait_ge(qk_normed, h * 2 + 2)
            pool.wait_ge(v_turned, h + 1)
            load_head(h + 1)
            pool.wait_ge(y_gated, h + 1)
            pool.dma_start(tiles_of(y_d, h), y_t[:, :].unsqueeze(1)).then_inc(y_stored, 16)
            pool.dma_start(z_s[:, :].unsqueeze(1), tiles_of(z_d, h + 1)).then_inc(z_in, 16)
            pool.wait_ge(y_stored, h * 16 + 16)
            pool.sem_inc(y_free, 1)
            store_gates(h + GATE_HEADS, 0, h + HEADS // 2)
        pool.wait_ge(y_gated, HEADS)
        pool.dma_start(y_d[HEADS - 1], y_t[:, :]).then_inc(y_stored, 16)
        store_gates(HEADS - 1 + GATE_HEADS, 0, HEADS - 1 + HEADS // 2)
        pool.wait_ge(y_stored, 16 * HEADS)

        for n, tile in enumerate(Y_ORDER):
            if n >= 4:
                pool.wait_ge(re_lo, n - 3)
            pool.dma_start(restg[n % 4][:, :], y_d[tile]).then_inc(restg_in[n % 4], 16)

        def load_gates(n, b):
            for g in range(2):
                pool.dma_start(gates[b][:, 2 * g:2 * g + 2, :], tiles_of(gate_d, n * 2 + KT * g, 2)).then_inc(gates_in[b], 16)

        for b in range(2):
            load_gates(b, b)
        with pool.Fori(1, BLOCKS // 2) as i:
            for b in range(2):
                pool.wait_ge(m_lo, i * 2 + (b - 1))
                load_gates(i * 2 + b, b)
        pool.wait_ge(slot_used, S_OUT)
        pool.dma_start(xs[:, :, :], xT.rearrange("(k p) n -> p k n", p=P)).then_inc(x_back, 16)
        for j in range(BLOCKS):
            pool.wait_ge(y_added[j % 4], 2 * CHUNKS + j // 4)
            pool.dma_start(outT[2 * j * P:2 * (j + 1) * P, :].rearrange("(a p) n -> p a n", p=P), xs[:, 2 * j:2 * j + 2, :]).then_inc(out_stored, 16)

    SPLIT_FREE = 16 * (ADA_A + 1)
    PAIRS = KT // 2

    @block.scalar
    def _(act):
        eps = par[:, EPSC:EPSC + 1]

        def split_hi(s, b):
            act.wait_ge(raw_full[b], (s - b) * 8 + SPLIT_FREE)
            act.wait_ge(slot_used, s - 1)
            act.activation(w_hi[b][:, :], raw[b][:, :], ACT.Copy).then_inc(hi_done, 1)

        def squares(n, b, tiles):
            if not isinstance(n, int) or n >= 2:
                act.wait_ge(sq_used, n - 1)
            act.activation(sq[b][:, :, :], xs[:, tiles, :], ACT.Square).then_inc(sq_done, 1)

        def inverse_root(n):
            act.wait_ge(sq_used, PAIRS * (n + 1))
            act.activation(lnb[:, :], bank[4][:, :], ACT.Ln, bias=eps, scale=1.0 / D).then_inc(ln_done, 1)
            act.wait_ge(ln_done, n + 1)
            act.activation(rstd[:, :], lnb[:, :], ACT.Exp, scale=-0.5).then_inc(rstd_done, 1)

        def norm(n, weights=False):
            shift = (SH1, SH2)[n]
            for k in range(KT):
                if weights and k in (2, 8):
                    b = k // 8
                    act.wait_ge(raw_full[b], SPLIT_FREE)
                    act.activation(w_hi[b][:, :], raw[b][:, :], ACT.Copy).then_inc(hi_done, 1)
                act.wait_ge(scaled_done, KT * n + k + 1)
                act.activation(act_hi[:, k, :], scaled[k % 4][:, :], ACT.Identity, bias=mod[:, shift + k:shift + k + 1]).then_inc(h_hi, 1)

        for started in (*evac, gate_out, ao_copied, *u_relu):
            act.sem_inc(started, 1)
        act.wait_ge(par_in, 16)
        act.activation(csilu[:, :], par[:, C_COL:C_COL + KT], ACT.Silu).then_inc(c_silu, 1)
        act.wait_ge(x_in, 16)
        for n in range(PAIRS):
            squares(n, n % 2, slice(2 * n, 2 * n + 2))
        inverse_root(0)
        norm(0, weights=True)

        act.wait_ge(h_lo, KT)
        act.wait_ge(pad_set, 2)

        def block_out(i, first, b, dst, func=ACT.Copy):
            act.wait_ge(slot_used, i * 4 + (4 * first + 2 * b + 2))
            for t in range(2):
                last = act.activation(dst[:, t, :], bank[2 * b + t][:, :], func)
            last.then_inc(evac[b], 1)

        with act.Fori(0, SW_BODIES) as i:
            for b in range(2):
                split_hi(i * 4 + (2 + 2 * b), 0)
                act.wait_ge(stg_free, i * 2 + (b + 1))
                block_out(i, 0, b, stg[b])
                split_hi(i * 4 + (3 + 2 * b), 1)
        with act.Fori(0, DN_BODIES) as i:
            for b in range(2):
                split_hi(i * 4 + (4 * SW_BODIES + 2 + 2 * b), 0)
                act.wait_ge(conv_step, i * 20 + 1)
                block_out(i, SW_BODIES, b, xpad[b][:, :, 2:2 + SEQ])
                split_hi(i * 4 + (4 * SW_BODIES + 3 + 2 * b), 1)
                act.wait_ge(conv_step, i * 20 + (b * 10 + 11))
                act.activation(stg[b][:, :, :], stg[b][:, :, :], ACT.Silu).then_inc(silu_done, 1)
        with act.Fori(0, Z_BODIES) as i:
            for b in range(2):
                first = SW_BODIES + DN_BODIES
                split_hi(i * 4 + (4 * first + 2 + 2 * b), 0)
                act.wait_ge(stg_free, i * 2 + (2 * first + b + 1))
                block_out(i, first, b, stg[b], ACT.Silu)
                split_hi(i * 4 + (4 * first + 3 + 2 * b), 1)

        act.wait_ge(sp_in, 32)
        act.activation(sp_hi[:, :], sp_raw[:, :], ACT.Copy).then_inc(sp_hi_done, 1)
        act.activation(e_alog[:, :], par[:, ALOG:ALOG + 16], ACT.Exp).then_inc(sp_act, 1)
        act.wait_ge(sp_summed, 1)
        act.activation(logits[:, :, :], chunked(bank[4][:, 0:NCH * 32]), ACT.Copy).then_inc(sp_act, 1)
        act.wait_ge(sp_act, 2)
        act.activation(e_beta[:, :, :], logits[:, :, 0:16], ACT.Exp, scale=-1.0).then_inc(sp_act, 1)
        act.wait_ge(sp_dve, 2)
        act.activation(a_exp[:, :, :], a_abs[:, :, :], ACT.Exp, scale=-1.0).then_inc(sp_act, 1)
        act.wait_ge(sp_act, 4)
        act.activation(a_ln[:, :, :], a_exp[:, :, :], ACT.Ln, bias=par[:, ONEC:ONEC + 1]).then_inc(sp_act, 1)
        act.wait_ge(cums_done, 1)
        for d in range(2):
            act.activation(g_cum[:, :, 8 * d:8 * d + 8], chunked(bank[5][:, 64 * d:64 * d + 64])[:, :, 8 * d:8 * d + 8], ACT.Copy).then_inc(sp_act, 1)
        act.activation(g_sum[:, :, :], chunked(bank[5][:, 128:192]), ACT.Copy).then_inc(sp_act, 1)
        act.wait_ge(sp_act, 8)
        act.activation(e_cum[:, :, :], g_cum[:, :, :], ACT.Exp).then_inc(sp_act, 1)
        act.activation(e_sum[:, :, :], g_sum[:, :, :], ACT.Exp).then_inc(sp_act, 1)
        act.wait_ge(sp_dve, SP_LEFT)
        act.activation(e_left[:, :, :], g_left[:, :, :], ACT.Exp).then_inc(sp_act, 1)

        def inverse_rms(n, scale=1.0 / P):
            act.wait_ge(aq_summed, n + 1)
            act.activation(q_ri[:, :], bank[2][:, :], ACT.Ln, bias=eps, scale=scale).then_inc(aq_ln, 1)
            act.wait_ge(aq_ln, n + 1)
            act.activation(q_ri[:, :], q_ri[:, :], ACT.Exp, scale=-0.5).then_inc(aq_rinv, 1)

        def gates_to_stage(n, b, free, at):
            act.wait_ge(slot_used, n * 2 + (S_ATT + 2))
            act.wait_ge(gst_free, free)
            for t in range(2):
                last = act.activation(gst[b][:, t, :], bank[at + t][:, :], ACT.Copy)
            last.then_inc(gate_out, 1)

        act.wait_ge(mask_in, 32)
        act.wait_ge(kv_in, 32 * KV_HEADS)
        for n in range(KV_HEADS):
            act.activation(q_sq[:, :], q_raw[n][:, :], ACT.Square).then_inc(aq_sq, 1)
            if n:
                act.wait_ge(aq_normed, n)
            inverse_rms(n)
            act.wait_ge(av_turned, n + 1)
            act.activation(v_tok[n][:, :, :], chunked(bank[4 + n][:, :]), ACT.Copy).then_inc(av_copied, 1)

        for kv in range(KV_HEADS):
            with act.Fori(0, 2) as i:
                for b in range(2):
                    h = i * 2 + (4 * kv + b)
                    act.wait_ge(q_in[b], i * 16 + (32 * kv + 16))
                    act.activation(q_sq[:, :], q_raw[b][:, :], ACT.Square).then_inc(aq_sq, 1)
                    act.wait_ge(aq_normed, h + KV_HEADS)
                    inverse_rms(h + KV_HEADS)
                    act.wait_ge(negated, h + 1)
                    for c in range(NCH):
                        act.activation(prob[:, c, :], prob[:, c, :], ACT.Exp, bias=s_neg[:, c:c + 1], accum_out=s_sum[:, c:c + 1]).then_inc(p_exp, 1)
                    act.wait_ge(p_step, h * 3 + 1)
                    act.activation(e_sink[:, :], s_sink[:, :], ACT.Exp).then_inc(sink_exp, 1)
                    split_hi(h * 2 + (S_ATT + 2), 0)
                    gates_to_stage(h, b, h + 1, 0)
                    act.wait_ge(ao_mm, h + 1)
                    act.wait_ge(a_free, h + 1)
                    act.activation(a_out[b][:, :], bank[4][:, :], ACT.Copy).then_inc(ao_copied, 1)
                    split_hi(h * 2 + (S_ATT + 3), 1)

        act.wait_ge(mask_in, 48)
        with act.Fori(0, HEADS) as h:
            act.wait_ge(head_in, h * 48 + 48)
            act.wait_ge(o_summed, h + 1)
            act.activation(nsq[0][:, :], qkv[:, 0, :], ACT.Square).then_inc(qk_sq, 1)
            act.wait_ge(o_normed, h + 1)
            act.activation(nsq[1][:, :], qkv[:, 1, :], ACT.Square).then_inc(qk_sq, 1)
            for k in range(2):
                act.wait_ge(qk_sum, h * 2 + k + 1)
                act.activation(nsq[k][:, :], bank[k][:, :], ACT.Ln, bias=eps).then_inc(qk_ln, 1)
                act.wait_ge(qk_ln, h * 2 + k + 1)
                if k == 0:
                    act.activation(nsq[k][:, :], nsq[k][:, :], ACT.Exp, scale=-0.5, bias=par[:, LNS:LNS + 1]).then_inc(qk_rinv, 1)
                else:
                    act.activation(nsq[k][:, :], nsq[k][:, :], ACT.Exp, scale=-0.5).then_inc(qk_rinv, 1)
            act.wait_ge(v_turned, h + 1)
            act.wait_ge(hs_set, h + 1)
            for d in range(2):
                for c in range(NCH):
                    last = act.activation(bv[d][:, c, :], bank[3][:, c * P:(c + 1) * P], ACT.Copy, scale=hs[:, d, SC_BETA, c:c + 1])
            last.then_inc(bv_done, 1)
            act.wait_ge(k_turned, h + 1)
            act.activation(k_tok[:, :, :], chunked(bank[2][:, :]), ACT.Copy).then_inc(ktok_done, 1)
            for d in range(2):
                act.wait_ge(exponents, h * 2 + d + 1)
                act.activation(aT[d][:, :, :], aT[d][:, :, :], ACT.Exp)
                act.activation(amat[d][:, :, :], amat[d][:, :, :], ACT.Exp, scale=-1.0)
                act.activation(qd[d][:, :, :], chunked(bank[2 + d][:, :]), ACT.Exp).then_inc(decays, 1)
            for d in range(2):
                act.wait_ge(x_turned, h * 2 + d + 1)
                act.activation(Xm[d][:, :, :], chunked(bank[2 + d][:, :]), ACT.Copy).then_inc(x_copied, 1)
            split_hi(h * 2 + (S_DELTA + 2), 0)
            for s in range(NCH):
                for d in range(2):
                    c = s if d == 0 else NCH - 1 - s
                    act.wait_ge(vn_mm[d], h * NCH + s + 1)
                    act.activation(vnew[d][:, :], bank[d][:, P:2 * P], ACT.Copy)
                    act.activation(vdec[d][:, :], bank[d][:, P:2 * P], ACT.Copy, scale=hs[:, d, SC_KD, c:c + 1]).then_inc(v_copied[d], 1)
            act.wait_ge(o_mm, h + 1)
            act.activation(o_t[:, :], bank[2][:, :], ACT.Copy).then_inc(of_copied, 1)
            act.wait_ge(o_sum, h + 1)
            act.activation(nsq[0][:, :], o_t[:, :], ACT.Square).then_inc(o_sq, 1)
            act.wait_ge(o_summed, h + 2)
            act.activation(nsq[1][:, :], bank[0][:, :], ACT.Ln, bias=eps, scale=1.0 / P).then_inc(o_ln, 1)
            act.wait_ge(o_ln, h + 1)
            act.activation(nsq[1][:, :], nsq[1][:, :], ACT.Exp, scale=-0.5).then_inc(o_rinv, 1)
            gates_to_stage(h + GATE_HEADS, 0, h + (GATE_HEADS + 2), 4)
            split_hi(h * 2 + (S_DELTA + 3), 1)

        for n, tile in enumerate(Y_ORDER):
            act.wait_ge(restg_in[n % 4], 16 * (n // 4 + 1))
            act.activation(y_hi[:, tile, :], restg[n % 4][:, :], ACT.Copy).then_inc(re_hi, 1)
        with act.Fori(0, BLOCKS // 2) as i:
            for b in range(2):
                act.wait_ge(gates_in[b], i * 32 + 32)
                act.activation(gates[b][:, :, :], gates[b][:, :, :], ACT.Sigmoid).then_inc(gates_open, 1)
                for j in range(2):
                    split_hi(i * 4 + (S_MERGE + 2 + 2 * b + j), j)
                act.wait_ge(m_full, i * 2 + (b + 1))
                act.activation(act_hi[:, bass.ds(i * 4 + 2 * b, 2), :], gates[b][:, 0:2, :], ACT.Copy).then_inc(m_hi, 1)

        def out_block(i, b):
            for j in range(2):
                split_hi(i * 4 + (S_OUT + 2 + 2 * b + j), j)
            act.wait_ge(x1_done, i * 2 + (b + 3))
            squares(i * 2 + (PAIRS + b), b, bass.ds(i * 4 + 2 * b, 2))

        with act.Fori(0, OUT_BODIES) as i:
            for b in range(2):
                out_block(i, b)
        inverse_root(1)
        norm(1)

        def mlp_in(c):
            with act.Fori(0, 2) as i:
                for b in range(2):
                    split_hi(c * 16 + i * 4 + (S_MLP + 2 + 2 * b), 0)
                    act.wait_ge(slot_used, c * 16 + i * 4 + (S_MLP + 2 * b + 2))
                    act.wait_ge(u_ready[b], c * 2 + i + 1)
                    for t in range(2):
                        last = act.activation(urelu[b][:, t, :], bank[2 * b + t][:, :], ACT.Relu)
                    last.then_inc(u_relu[b], 1)
                    act.wait_ge(u_sq, c * 4 + i * 2 + (b + 1))
                    act.activation(u_hi[:, bass.ds(i * 4 + 2 * b, 2), :], urelu[b][:, :, :], ACT.Copy).then_inc(u_high, 1)
                    split_hi(c * 16 + i * 4 + (S_MLP + 3 + 2 * b), 1)

        with act.Fori(0, CHUNKS - 1) as c:
            mlp_in(c)
            with act.Fori(0, 2) as i:
                for j in range(4):
                    split_hi(c * 16 + i * 4 + (S_MLP + 10 + j), j % 2)
        mlp_in(CHUNKS - 1)
        for j in range(6):
            split_hi(16 * (CHUNKS - 1) + S_MLP + 10 + j, j % 2)

    @block.vector
    def _(dve):
        def split_lo(s, b):
            dve.wait_ge(hi_done, s + 1)
            dve.tensor_tensor(w_lo[b][:, :], raw[b][:, :], w_hi[b][:, :].bitcast(FP32), ALU.subtract).then_inc(lo_done, 1)

        def ada_slot(g, j, acc, b, landed, free):
            dve.wait_ge(raw_full[b], landed)
            if j == 0:
                dve.wait_ge(ada_summed, free)
            for k in range(4):
                m = 4 * j + k
                src = raw[b][:, k * 512:(k + 1) * 512]
                if m == 0:
                    dve.tensor_scalar(acc[:, :], src, csilu[:, 0:1], None, ALU.mult).then_inc(ada_step, 1)
                else:
                    dve.wait_ge(ada_step, g * 16 + m)
                    dve.scalar_tensor_tensor(out=acc[:, :], in0=src, scalar=csilu[:, m:m + 1], in1=acc[:, :], op0=ALU.mult, op1=ALU.add).then_inc(ada_step, 1)

        def ada_finish(g0, g1):
            dve.wait_ge(ada_summed, g1 + 2)
            dve.tensor_tensor(mod[:, 4 * g0:4 * g1], bank[7][:, 4 * g0:4 * g1], par[:, BADA + 4 * g0:BADA + 4 * g1], ALU.add).then_inc(mod_done, 1)

        def norm(n, weights=False):
            nw, scale, shift = ((N1W, SC1, SH1), (N2W, SC2, SH2))[n]
            dve.scalar_tensor_tensor(out=gain[:, n, :], in0=mod[:, scale:scale + KT], scalar=1.0, in1=par[:, nw:nw + KT], op0=ALU.add, op1=ALU.mult).then_inc(gain_done, 1)
            dve.wait_ge(gain_done, n + 1)
            dve.wait_ge(rstd_done, n + 1)
            for k in range(KT + 1):
                if weights and k in (4, 10):
                    split_lo(k // 8, k // 8)
                if k < KT:
                    if k >= 4:
                        dve.wait_ge(h_lo, KT * n + k - 3)
                    dve.scalar_tensor_tensor(out=scaled[k % 4][:, :], in0=xs[:, k, :], scalar=gain[:, n, k:k + 1], in1=rstd[:, :], op0=ALU.mult, op1=ALU.mult).then_inc(scaled_done, 1)
                if k:
                    j = k - 1
                    dve.wait_ge(h_hi, KT * n + j + 1)
                    dve.scalar_tensor_tensor(out=act_lo[:, j, :], in0=scaled[j % 4][:, :], scalar=mod[:, shift + j:shift + j + 1], in1=act_hi[:, j, :].bitcast(FP32), op0=ALU.add, op1=ALU.subtract).then_inc(h_lo, 1)

        for started in (conv_step, *p_copied, o_normed, *merged, x1_done, x1_done, *u_ready, *y_added):
            dve.sem_inc(started, 1)
        dve.wait_ge(par_in, 16)
        dve.wait_ge(c_silu, 1)
        with dve.Fori(0, ADA_A // 2) as i:
            for n in range(2):
                for j in range(4):
                    g = i * 2 + n
                    ada_slot(g, j, ada_acc[n], j, g * 16 + 16, g + 1)
        ada_finish(0, ADA_A)
        dve.wait_ge(mod_done, 1)
        dve.wait_ge(x_in, 16)
        norm(0, weights=True)

        def ada_beside(g, q):
            n, j = q // 4, q % 4
            g = g + n
            ada_slot(g, j, ada_acc[n], 2 + j % 2, (g - ADA_A) * 32 + 16 * (ADA_A + 1 + j // 2), g + (2 - n))

        with dve.Fori(0, SW_BODIES) as i:
            for j in range(4):
                for q in (2 * j, 2 * j + 1):
                    ada_beside(i * 2 + ADA_A, q)
                split_lo(i * 4 + (2 + j), j % 2)
        with dve.Fori(0, DN_BODIES) as i:
            for b in range(2):
                for j in range(2):
                    ada_beside(i + ADA_DN, 2 * b + j)
                    split_lo(i * 4 + (4 * SW_BODIES + 2 + 2 * b + j), j)
                dve.wait_ge(evac[b], i + (SW_BODIES + 2))
                dve.wait_ge(stg_free, i * 2 + (2 * SW_BODIES + b + 1))
                for k in range(CONV_K):
                    for t in range(2):
                        tap = par[:, bass.ds(i * 20 + (CONVW + (2 * b + t) * CONV_K + k), 1)]
                        src = xpad[b][:, t, k:k + SEQ]
                        if k == 0:
                            dve.tensor_scalar(stg[b][:, t, :], src, tap, None, ALU.mult).then_inc(conv_step, 1)
                        else:
                            dve.wait_ge(conv_step, i * 20 + (10 * b + 2 * k + t))
                            dve.scalar_tensor_tensor(out=stg[b][:, t, :], in0=src, scalar=tap, in1=stg[b][:, t, :], op0=ALU.mult, op1=ALU.add).then_inc(conv_step, 1)
        with dve.Fori(0, Z_BODIES) as i:
            for j in range(4):
                for q in (2 * j, 2 * j + 1):
                    ada_beside(i * 2 + ADA_Z, q)
                split_lo(i * 4 + (4 * (SW_BODIES + DN_BODIES) + 2 + j), j % 2)
        ada_finish(ADA_A, ADA_G)

        n_sp = [0]

        def kept(ins):
            n_sp[0] += 1
            ins.then_inc(sp_dve, 1)

        dve.wait_ge(sp_hi_done, 1)
        dve.tensor_tensor(sp_lo[:, :], sp_raw[:, :], sp_hi[:, :].bitcast(FP32), ALU.subtract).then_inc(sp_lo_done, 1)
        dve.wait_ge(sp_act, 2)
        kept(dve.tensor_tensor(a_raw[:, :, :], logits[:, :, 16:32], par[:, DTB:DTB + 16].unsqueeze(1).to_broadcast([P, NCH, 16]), ALU.add))
        dve.wait_ge(sp_dve, 1)
        kept(dve.scalar_tensor_tensor(out=a_abs[:, :, :], in0=a_raw[:, :, :], scalar=-1.0, in1=a_raw[:, :, :], op0=ALU.mult, op1=ALU.max))
        dve.wait_ge(sp_act, 3)
        kept(dve.tensor_scalar(e_beta[:, :, :], e_beta[:, :, :], 1.0, None, ALU.add))
        dve.wait_ge(sp_dve, 3)
        kept(dve.reciprocal(e_beta[:, :, :], e_beta[:, :, :]))
        dve.wait_ge(sp_act, 5)
        kept(dve.scalar_tensor_tensor(out=a_soft[:, :, :], in0=a_raw[:, :, :], scalar=0.0, in1=a_ln[:, :, :], op0=ALU.max, op1=ALU.add))
        dve.wait_ge(sp_dve, 5)
        kept(dve.scalar_tensor_tensor(out=g_tok[:, :, :], in0=a_soft[:, :, :], scalar=-1.0, in1=e_alog[:, :].unsqueeze(1).to_broadcast([P, NCH, 16]), op0=ALU.mult, op1=ALU.mult))
        assert n_sp[0] == SP_G
        dve.wait_ge(sp_act, 8)
        kept(dve.tensor_tensor(g_left[:, :, :], g_sum[:, :, :], g_cum[:, :, :], ALU.subtract))
        assert n_sp[0] == SP_LEFT
        dve.wait_ge(sp_act, 10)
        dve.wait_ge(sp_dve, 4)
        kept(dve.scalar_tensor_tensor(out=nbe[:, :, :], in0=e_cum[:, :, :], scalar=-1.0, in1=e_beta[:, :, :], op0=ALU.mult, op1=ALU.mult))
        dve.wait_ge(sp_act, SP_ACT_ALL)
        dve.wait_ge(sp_dve, n_sp[0])
        for kind, src in ((SC_G, g_tok), (SC_GC, g_cum), (SC_BETA, e_beta), (SC_NBE, nbe), (SC_KD, e_left), (SC_EGL, e_sum)):
            for d in range(2):
                kept(dve.tensor_copy(scal[:, :, d, kind, :], src[:, :, 8 * d:8 * d + 8].rearrange("p c h -> p h c")))
        assert n_sp[0] == SP_DVE_ALL

        def norm_and_rotate(n, src, weight, out):
            dve.wait_ge(aq_rinv, n + 1)
            dve.scalar_tensor_tensor(out=out[:, :], in0=src[:, :], scalar=par[:, weight:weight + 1], in1=q_ri[:, :], op0=ALU.mult, op1=ALU.mult).then_inc(aq_normed, 1)
            dve.wait_ge(aq_turned, n + 1)
            q = 2 * (P // 8)
            dve.tensor_tensor(rtmp[0:q, :], bank[3][0:q, :], sin_t[0:q, :], ALU.mult).then_inc(aq_step, 1)
            dve.tensor_tensor(out[0:q, :], out[0:q, :], cos_t[0:q, :], ALU.mult).then_inc(aq_step, 1)
            dve.wait_ge(aq_step, n * 2 + 2)
            dve.tensor_tensor(out[0:q, :], out[0:q, :], rtmp[0:q, :], ALU.add).then_inc(aq_roped, 1)

        dve.wait_ge(mask_in, 32)
        for n in range(KV_HEADS):
            norm_and_rotate(n, q_raw[n], KNW, k_fin[n])
        for kv in range(KV_HEADS):
            with dve.Fori(0, 2) as i:
                for b in range(2):
                    h = i * 2 + (4 * kv + b)
                    dve.wait_ge(scores_mm, h + 1)
                    norm_and_rotate(h + KV_HEADS, q_raw[b], QNW, q_nrm)
                    dve.wait_ge(scores_mm, h + 2)
                    for c in range(NCH):
                        lo, hi = (P if c == 0 else 0), (2 * P if c == NCH - 1 else 3 * P)
                        dve.scalar_tensor_tensor(out=prob[:, c, lo:hi], in0=bank[4 + c][:, lo:hi], scalar=SCALE, in1=am[:, lo // P:hi // P, :].rearrange("p a n -> p (a n)"), op0=ALU.mult, op1=ALU.add).then_inc(scored, 1)
                    for c in (0, NCH - 1):
                        off = 0 if c == 0 else 2 * P
                        dve.memset(prob[:, c, off:off + P], -1e30).then_inc(scored, 1)
                    dve.wait_ge(scored, h * 6 + 6)
                    dve.tensor_reduce(s_max[:, :], prob[:, :, :], axis=AX.X, op=ALU.max).then_inc(maxed, 1)
                    dve.wait_ge(maxed, h + 1)
                    sink = par[:, bass.ds(SINK + h, 1)]
                    dve.tensor_scalar(s_neg[:, :], s_max[:, :], sink, -1.0, ALU.max, ALU.mult).then_inc(negated, 1)
                    dve.wait_ge(negated, h + 1)
                    dve.tensor_scalar(s_sink[:, :], s_neg[:, :], sink, None, ALU.add).then_inc(p_step, 1)
                    split_lo(h * 2 + (S_ATT + 2), 0)
                    dve.wait_ge(sink_exp, h + 1)
                    dve.wait_ge(p_exp, h * NCH + NCH)
                    dve.tensor_tensor(s_inv[:, :], s_sum[:, :], e_sink[:, :], ALU.add).then_inc(p_step, 1)
                    dve.wait_ge(p_step, h * 3 + 2)
                    dve.reciprocal(s_inv[:, :], s_inv[:, :]).then_inc(p_step, 1)
                    dve.wait_ge(p_step, h * 3 + 3)
                    for c in range(NCH):
                        dve.tensor_scalar(prob[:, c, :], prob[:, c, :], s_inv[:, c:c + 1], None, ALU.mult).then_inc(p_ready, 1)
                    for c in range(NCH):
                        dve.wait_ge(p_turned, h * NCH + c + 1)
                        dve.tensor_copy(prob_t[:, c, :], bank[2 + c % 2][:, 0:3 * P]).then_inc(p_copied[c % 2], 1)
                    split_lo(h * 2 + (S_ATT + 3), 1)

        dve.wait_ge(mask_in, 48)

        def every(m):
            return dm[:, m, :].unsqueeze(1).to_broadcast([P, NCH, P])

        with dve.Fori(0, HEADS) as h:
            dve.tensor_copy(hs[:, :, :, :].rearrange("p d k c -> p (d k c)"), scal[:, bass.ds(h, 1), :, :, :].rearrange("p h d k c -> p (h d k c)")).then_inc(hs_set, 1)
            for k, dst in enumerate((qn, kn)):
                dve.wait_ge(qk_rinv, h * 2 + k + 1)
                dve.tensor_tensor(dst[:, :], qkv[:, k, :], nsq[k][:, :], ALU.mult).then_inc(qk_normed, 1)
            dve.wait_ge(hs_set, h + 1)
            for d in range(2):
                dve.wait_ge(gb_done, h * 2 + d + 1)
                for c in range(NCH):
                    for out, keep in ((aT[d], M_KEEP_T + d), (amat[d], M_KEEP + d)):
                        last = dve.scalar_tensor_tensor(out=out[:, c, :], in0=bank[2 + d][:, c * P:(c + 1) * P], scalar=hs[:, d, SC_GC, c:c + 1], in1=dm[:, keep, :], op0=ALU.subtract, op1=ALU.add)
                last.then_inc(exponents, 1)
            dve.wait_ge(grams, h + 1)
            for d in range(2):
                dve.wait_ge(decays, h * 2 + d + 1)
                for c in range(NCH):
                    last = dve.scalar_tensor_tensor(out=amat[d][:, c, :], in0=bank[0][:, c * P:(c + 1) * P], scalar=hs[:, d, SC_BETA, c:c + 1], in1=amat[d][:, c, :], op0=ALU.mult, op1=ALU.mult)
                last.then_inc(a_made, 1)
                dve.wait_ge(a_made, h * 4 + 2 * d + 1)
                dve.tensor_tensor(Tm[d][:, :, :], amat[d][:, :, :], every(M_LVL + d), ALU.mult).then_inc(t_first, 1)
                dve.wait_ge(t_first, h * 2 + d + 1)
                dve.tensor_tensor(Tm[d][:, :, :], every(M_IDENT), Tm[d][:, :, :], ALU.subtract).then_inc(t_made, 1)
                dve.tensor_tensor(aT[d][:, :, :], chunked(bank[1][:, :]), aT[d][:, :, :], ALU.mult)
                dve.tensor_tensor(qd[d][:, :, :], chunked(qn[:, :]), qd[d][:, :, :], ALU.mult).then_inc(a_made, 1)
            for lvl in range(1, LEVELS):
                m = lvl - 1
                for d in range(2):
                    dve.wait_ge(y_mm[d], h * 6 + m + 1)
                    dve.tensor_tensor(Ym[d][:, :, :], chunked(bank[2 + d][:, :]), every(M_LVL + 2 * lvl + 1 - d), ALU.mult).then_inc(y_masked[d], 1)
                for d in range(2):
                    dve.wait_ge(xp_mm[d], h * 6 + m + 1)
                    if lvl == 1:
                        dve.wait_ge(x_copied, h * 2 + d + 1)
                    else:
                        dve.wait_ge(x_upd[d], h * 6 + m)
                    dve.tensor_tensor(Xm[d][:, :, :], Xm[d][:, :, :], chunked(bank[d][:, :]), ALU.subtract).then_inc(x_upd[d], 1)
                    if lvl < LEVELS - 1:
                        dve.wait_ge(tp_mm[d], h * 5 + m + 1)
                        if lvl == 1:
                            dve.wait_ge(t_made, h * 2 + d + 1)
                        else:
                            dve.wait_ge(t_upd[d], h * 5 + m)
                        dve.tensor_tensor(Tm[d][:, :, :], Tm[d][:, :, :], chunked(bank[2 + d][:, :]), ALU.subtract).then_inc(t_upd[d], 1)
                if lvl == LEVELS - 2:
                    split_lo(h * 2 + (S_DELTA + 2), 0)
            dve.wait_ge(bv_done, h + 1)
            for s in range(NCH):
                for d in range(2):
                    c = s if d == 0 else NCH - 1 - s
                    if s:
                        dve.wait_ge(ks_mm[d], h * 3 + s)
                        dve.scalar_tensor_tensor(out=resid[d][:, :], in0=bank[d][:, 0:P], scalar=hs[:, d, SC_NBE, c:c + 1], in1=bv[d][:, c, :], op0=ALU.mult, op1=ALU.add).then_inc(resid_done[d], 1)
                for d in range(2):
                    c = s if d == 0 else NCH - 1 - s
                    if s < NCH - 1:
                        dve.wait_ge(kv_mm[d], h * 3 + s + 1)
                        kv = bank[d][:, 2 * P:3 * P]
                        if s == 0:
                            dve.tensor_copy(state[d][:, :], kv).then_inc(state_upd[d], 1)
                        else:
                            dve.wait_ge(state_upd[d], h * 3 + s)
                            dve.scalar_tensor_tensor(out=state[d][:, :], in0=state[d][:, :], scalar=hs[:, d, SC_EGL, c:c + 1], in1=kv, op0=ALU.mult, op1=ALU.add).then_inc(state_upd[d], 1)
            dve.wait_ge(of_copied, h + 1)
            dve.tensor_tensor(o_t[:, :], bank[3][:, :], o_t[:, :], ALU.add).then_inc(o_sum, 1)
            dve.wait_ge(o_rinv, h + 1)
            dve.wait_ge(o_sum, h + 1)
            dve.scalar_tensor_tensor(out=o_t[:, :], in0=o_t[:, :], scalar=par[:, ONW:ONW + 1], in1=nsq[1][:, :], op0=ALU.mult, op1=ALU.mult).then_inc(o_normed, 1)
            dve.wait_ge(o_normed, h + 2)
            dve.wait_ge(z_in, h * 16 + 16)
            dve.wait_ge(y_free, h + 1)
            dve.tensor_tensor(y_t[:, :], o_t[:, :], z_s[:, :], ALU.mult).then_inc(y_gated, 1)
            split_lo(h * 2 + (S_DELTA + 3), 1)

        for n, tile in enumerate(Y_ORDER):
            dve.wait_ge(re_hi, n + 1)
            dve.tensor_tensor(y_lo[:, tile, :], restg[n % 4][:, :], y_hi[:, tile, :].bitcast(FP32), ALU.subtract).then_inc(re_lo, 1)
        with dve.Fori(0, BLOCKS // 2) as i:
            for b in range(2):
                first = 2 * b + S_MERGE
                split_lo(i * 4 + (first + 2), 0)
                dve.wait_ge(gates_open, i * 2 + (b + 1))
                dve.wait_ge(slot_used, i * 4 + (first + 1))
                for t in range(2):
                    dve.tensor_tensor(gates[b][:, 2 + t, :], bank[4 * b + t][:, :], gates[b][:, 2 + t, :], ALU.mult)
                split_lo(i * 4 + (first + 3), 1)
                dve.wait_ge(slot_used, i * 4 + (first + 2))
                for t in range(2):
                    last = dve.tensor_tensor(gates[b][:, t, :], bank[4 * b + 2 + t][:, :], gates[b][:, t, :], ALU.mult)
                last.then_inc(merged[b], 1)
                dve.wait_ge(merged[b], i + 2)
                dve.tensor_tensor(gates[b][:, 0:2, :], gates[b][:, 0:2, :], gates[b][:, 2:4, :], ALU.add).then_inc(m_full, 1)
                dve.wait_ge(m_hi, i * 2 + (b + 1))
                dve.wait_ge(m_full, i * 2 + (b + 1))
                at = bass.ds(i * 4 + 2 * b, 2)
                dve.tensor_tensor(act_lo[:, at, :], gates[b][:, 0:2, :], act_hi[:, at, :].bitcast(FP32), ALU.subtract).then_inc(m_lo, 1)

        dve.wait_ge(mod_done, 2)
        dve.wait_ge(x_back, 16)
        with dve.Fori(0, OUT_BODIES) as i:
            for b in range(2):
                for j in range(2):
                    split_lo(i * 4 + (S_OUT + 2 + 2 * b + j), j)
                dve.wait_ge(slot_used, i * 4 + (S_OUT + 2 * b + 2))
                for t in range(2):
                    k = i * 4 + (2 * b + t)
                    tile = xs[:, bass.ds(k, 1), :].rearrange("p a n -> p (a n)")
                    last = dve.scalar_tensor_tensor(out=tile, in0=bank[2 * b + t][:, :], scalar=mod[:, bass.ds(k + GA1, 1)], in1=tile, op0=ALU.mult, op1=ALU.add)
                last.then_inc(x1_done, 1)
        dve.wait_ge(x1_done, 2 * OUT_BODIES + 2)
        norm(1)

        def mlp_in(c):
            with dve.Fori(0, 2) as i:
                for b in range(2):
                    split_lo(c * 16 + i * 4 + (S_MLP + 2 + 2 * b), 0)
                    dve.wait_ge(u_relu[b], c * 2 + i + 2)
                    dve.tensor_tensor(urelu[b][:, :, :], urelu[b][:, :, :], urelu[b][:, :, :], ALU.mult).then_inc(u_sq, 1)
                    dve.wait_ge(u_sq, c * 4 + i * 2 + (b + 1))
                    dve.wait_ge(u_high, c * 4 + i * 2 + (b + 1))
                    dve.tensor_tensor(u_lo[:, bass.ds(i * 4 + 2 * b, 2), :], urelu[b][:, :, :], u_hi[:, bass.ds(i * 4 + 2 * b, 2), :].bitcast(FP32), ALU.subtract).then_inc(u_ready[b], 1)
                    split_lo(c * 16 + i * 4 + (S_MLP + 3 + 2 * b), 1)

        def mlp_out(c, i, j, split=True):
            if split:
                split_lo(c * 16 + i * 4 + (S_MLP + 10 + j), j % 2)
            dve.wait_ge(slot_used, c * 16 + i * 4 + (S_MLP + 9 + j))
            dve.wait_ge(y_added[j], c * 2 + i + 1)
            for t in range(2):
                k = i * 8 + (2 * j + t)
                tile = xs[:, bass.ds(k, 1), :].rearrange("p a n -> p (a n)")
                last = dve.scalar_tensor_tensor(out=tile, in0=bank[2 * j + t][:, :], scalar=mod[:, bass.ds(k + GA2, 1)], in1=tile, op0=ALU.mult, op1=ALU.add)
            last.then_inc(y_added[j], 1)

        with dve.Fori(0, CHUNKS - 1) as c:
            mlp_in(c)
            with dve.Fori(0, 2) as i:
                for j in range(4):
                    mlp_out(c, i, j)
        mlp_in(CHUNKS - 1)
        for i in range(2):
            for j in range(4):
                mlp_out(CHUNKS - 1, i, j, split=4 * i + j < 6)

    @block.tensor
    def _(pe):
        def slot(s, b, banks, hi, lo, k0, first, last, ready=None):
            pe.wait_ge(lo_done, s + 1)
            for k in range(ROWS):
                if ready:
                    ready(k)
                for t in range(2):
                    w = slice(k * COLS + t * P, k * COLS + (t + 1) * P)
                    pe.matmul(banks[t][:, :], w_hi[b][:, w], hi[:, k0 + k, :], start=first and k == 0, stop=False)
                    pe.matmul(banks[t][:, :], w_hi[b][:, w], lo[:, k0 + k, :], start=False, stop=False)
                    end = pe.matmul(banks[t][:, :], w_lo[b][:, w], hi[:, k0 + k, :], start=False, stop=last and k == ROWS - 1)
            end.then_inc(slot_used, 1)

        def gate_rows(n, a, z, at):
            for u in range(a, z):
                j, k = divmod(u, ROWS)
                if u == 0:
                    pe.wait_ge(gate_out, n + 1)
                if k == 0:
                    pe.wait_ge(lo_done, n * 2 + (S_ATT + j + 1))
                for t in range(2):
                    w = slice(k * COLS + t * P, k * COLS + (t + 1) * P)
                    pe.matmul(bank[at + t][:, :], w_hi[j][:, w], act_hi[:, u, :], start=u == 0, stop=False)
                    pe.matmul(bank[at + t][:, :], w_hi[j][:, w], act_lo[:, u, :], start=False, stop=False)
                    end = pe.matmul(bank[at + t][:, :], w_lo[j][:, w], act_hi[:, u, :], start=False, stop=u == KT - 1)
                if k == ROWS - 1:
                    end.then_inc(slot_used, 1)

        def ada_sum(g, acc):
            pe.wait_ge(ada_step, g * 16 + 16)
            for j in range(4):
                last = pe.matmul(bank[7][:, bass.ds(g * 4 + j, 1)], acc[:, j * P:(j + 1) * P], ones[:, 0:1], start=True, stop=True)
            last.then_inc(ada_summed, 1)

        def sum_squares(n, b, start=False, stop=False):
            pe.wait_ge(sq_done, n + 1)
            for t in range(2):
                mm = pe.matmul(bank[4][:, :], ones[:, :], sq[b][:, t, :], start=start and t == 0, stop=stop and t == 1)
            mm.then_inc(sq_used, 1)

        for started in (scores_mm, o_summed):
            pe.sem_inc(started, 1)
        pe.sem_inc(ada_summed, 2)
        pe.wait_ge(ones_set, 1)
        for n in range(KT // 2):
            sum_squares(n, n % 2, n == 0, n == KT // 2 - 1)
        with pe.Fori(0, ADA_A // 2) as i:
            for n in range(2):
                ada_sum(i * 2 + n, ada_acc[n])

        def projections(first, bodies, g, groups):
            with pe.Fori(0, bodies) as i:
                for b in range(2):
                    pe.wait_ge(evac[b], i + (first + 1))
                    for j in range(2):

                        def ready(k):
                            if first == 0 and b == 0:
                                pe.wait_ge(h_lo, ROWS * j + k + 1)

                        slot(i * 4 + (4 * first + 2 * b + j), j, bank[2 * b:2 * b + 2], act_hi, act_lo, ROWS * j, j == 0, j == 1, ready)
                for n in range(groups):
                    ada_sum(i * groups + (g + n), ada_acc[n])

        projections(0, SW_BODIES, ADA_A, 2)
        projections(SW_BODIES, DN_BODIES, ADA_DN, 1)
        projections(SW_BODIES + DN_BODIES, Z_BODIES, ADA_Z, 2)

        pe.wait_ge(sp_lo_done, 1)
        for c in range(NCH):
            out = bank[4][:, 32 * c:32 * c + 32]
            for k in range(KT):
                tok = slice(c * P, (c + 1) * P)
                w = slice(32 * k, 32 * k + 32)
                pe.matmul(out, act_hi[:, k, tok], sp_hi[:, w], start=k == 0, stop=False)
                pe.matmul(out, act_lo[:, k, tok], sp_hi[:, w], start=False, stop=False)
                last = pe.matmul(out, act_hi[:, k, tok], sp_lo[:, w], start=False, stop=k == KT - 1)
        last.then_inc(sp_summed, 1)
        pe.wait_ge(sp_dve, SP_G)
        for n, m in enumerate((tri[:, 0, :], tri[:, 1, :], ones[:, :])):
            last = pe.matmul(bank[5][:, 64 * n:64 * n + 64], m, g_tok[:, :, :].rearrange("p c n -> p (c n)"), start=True, stop=True)
        last.then_inc(cums_done, 1)

        def rotate(n, q, fill=None):
            pe.wait_ge(aq_sq, n + 1)
            pe.matmul(bank[2][:, :], ones[:, :], q_sq[:, :], start=True, stop=True).then_inc(aq_summed, 1)
            if fill is not None:
                gate_rows(fill, 0, 2, 0)
            pe.wait_ge(aq_normed, n + 1)
            pe.matmul(bank[3][:, :], rot_m, q[:, :], start=True, stop=True).then_inc(aq_turned, 1)
            if fill is not None:
                gate_rows(fill, 2, 4, 0)

        pe.wait_ge(mask_in, 32)
        pe.wait_ge(kv_in, 32 * KV_HEADS)
        for b in range(2):
            pe.wait_ge(evac[b], SW_BODIES + DN_BODIES + Z_BODIES + 1)
        pe.wait_ge(mod_done, 2)
        for n in range(KV_HEADS):
            for c in range(NCH):
                last = pe.transpose(bank[4 + n][:, c * P:(c + 1) * P], v_raw[n][:, c * P:(c + 1) * P], a_id[:, :])
            last.then_inc(av_turned, 1)
            rotate(n, k_fin[n])
            pe.wait_ge(aq_roped, n + 1)
        pe.wait_ge(av_copied, KV_HEADS)
        for kv in range(KV_HEADS):
            with pe.Fori(0, 2) as i:
                for b in range(2):
                    h = i * 2 + (4 * kv + b)
                    rotate(h + KV_HEADS, q_nrm, h)
                    pe.wait_ge(aq_roped, h + KV_HEADS + 1)
                    pe.wait_ge(ao_copied, h + 1)
                    for c in range(NCH):
                        lo, hi = max(c - 1, 0), min(c + 2, NCH)
                        last = pe.matmul(bank[4 + c][:, (lo - c + 1) * P:(hi - c + 1) * P], q_nrm[:, c * P:(c + 1) * P], k_fin[kv][:, lo * P:hi * P], start=True, stop=True)
                    last.then_inc(scores_mm, 1)
                    gate_rows(h, 4, 13, 0)
                    for c in range(NCH):
                        pe.wait_ge(p_ready, h * NCH + c + 1)
                        pe.wait_ge(p_copied[c % 2], h * 2 + c // 2 + 1)
                        for j in range(3):
                            last = pe.transpose(bank[2 + c % 2][:, j * P:(j + 1) * P], prob[:, c, j * P:(j + 1) * P], a_id[:, :])
                        last.then_inc(p_turned, 1)
                    gate_rows(h, 13, 16, 0)
                    for c in range(NCH):
                        pe.wait_ge(p_copied[c % 2], h * 2 + c // 2 + 2)
                        keys = [j for j in range(3) if 0 <= c + j - 1 < NCH]
                        for j in keys:
                            last = pe.matmul(bank[4][:, c * P:(c + 1) * P], v_tok[kv][:, c + j - 1, :], prob_t[:, c, j * P:(j + 1) * P], start=j == keys[0], stop=j == keys[-1])
                    last.then_inc(ao_mm, 1)

        pe.wait_ge(mask_in, 48)
        ident = dm[:, M_IDENT, :]

        def part(t, c):
            return t[:, c * P:(c + 1) * P]

        with pe.Fori(0, HEADS) as h:
            pe.wait_ge(head_in, h * 48 + 48)
            for c in range(NCH):
                last = pe.transpose(part(bank[3], c), qkv[:, 2, c * P:(c + 1) * P], ident)
            last.then_inc(v_turned, 1)
            for k in range(2):
                pe.wait_ge(qk_sq, h * 2 + k + 1)
                pe.matmul(bank[k][:, :], ones[:, :], nsq[k][:, :], start=True, stop=True).then_inc(qk_sum, 1)
            gate_rows(h + GATE_HEADS, 0, 2, 4)
            pe.wait_ge(qk_normed, h * 2 + 2)
            for c in range(NCH):
                last = pe.transpose(part(bank[2], c), part(kn, c), ident)
            last.then_inc(k_turned, 1)
            for c in range(NCH):
                pe.matmul(part(bank[0], c), part(kn, c), part(kn, c), start=True, stop=True)
            for c in range(NCH):
                last = pe.matmul(part(bank[1], c), part(kn, c), part(qn, c), start=True, stop=True)
            last.then_inc(grams, 1)
            pe.wait_ge(hs_set, h + 1)
            for d in (0, 1):
                pe.wait_ge(ktok_done, h + 1)
                for c in range(NCH):
                    last = pe.matmul(part(bank[2 + d], c), hs[:, d, SC_G, c:c + 1].to_broadcast([P, P]), dm[:, M_LE + d, :], start=True, stop=True)
                last.then_inc(gb_done, 1)
            gate_rows(h + GATE_HEADS, 2, 5, 4)
            for d in range(2):
                pe.wait_ge(t_made, h * 2 + d + 1)
                for c in range(NCH):
                    last = pe.transpose(part(bank[2 + d], c), Tm[d][:, c, :], ident)
                last.then_inc(x_turned, 1)
            for lvl in range(1, LEVELS):
                m = lvl - 1
                for d in range(2):
                    if lvl == 1:
                        pe.wait_ge(x_copied, h * 2 + d + 1)
                    else:
                        pe.wait_ge(x_upd[d], h * 6 + m)
                        pe.wait_ge(t_upd[d], h * 5 + m)
                    for c in range(NCH):
                        last = pe.matmul(part(bank[2 + d], c), amat[d][:, c, :], Xm[d][:, c, :], start=True, stop=True)
                    last.then_inc(y_mm[d], 1)
                gate_rows(h + GATE_HEADS, lvl + 4, lvl + 5, 4)
                if lvl == 1:
                    pe.wait_ge(a_made, h * 4 + 4)
                for d in range(2):
                    pe.wait_ge(y_masked[d], h * 6 + m + 1)
                    for c in range(NCH):
                        last = pe.matmul(part(bank[d], c), Tm[d][:, c, :], Ym[d][:, c, :], start=True, stop=True)
                    last.then_inc(xp_mm[d], 1)
                    if lvl < LEVELS - 1:
                        for c in range(NCH):
                            last = pe.matmul(part(bank[2 + d], c), Ym[d][:, c, :], Tm[d][:, c, :], start=True, stop=True)
                        last.then_inc(tp_mm[d], 1)
            for s in range(NCH):
                for d in range(2):
                    c = s if d == 0 else NCH - 1 - s
                    if s:
                        pe.wait_ge(state_upd[d], h * 3 + s)
                        pe.matmul(bank[d][:, 0:P], part(kn, c), state[d][:, :], start=True, stop=True).then_inc(ks_mm[d], 1)
                for d in range(2):
                    c = s if d == 0 else NCH - 1 - s
                    if s:
                        pe.wait_ge(resid_done[d], h * 3 + s)
                        rhs = resid[d][:, :]
                    else:
                        pe.wait_ge(bv_done, h + 1)
                        pe.wait_ge(x_upd[d], h * 6 + 6)
                        rhs = bv[d][:, c, :]
                    pe.matmul(bank[d][:, P:2 * P], Xm[d][:, c, :], rhs, start=True, stop=True).then_inc(vn_mm[d], 1)
                gate_rows(h + GATE_HEADS, s + 11, s + 12, 4)
                for d in range(2):
                    c = s if d == 0 else NCH - 1 - s
                    if s:
                        pe.matmul(part(bank[2 + d], c), state[d][:, :], qd[d][:, c, :], start=True, stop=False)
                    pe.wait_ge(v_copied[d], h * NCH + s + 1)
                    last = pe.matmul(part(bank[2 + d], c), vnew[d][:, :], aT[d][:, c, :], start=s == 0, stop=True)
                    if s < NCH - 1:
                        pe.matmul(bank[d][:, 2 * P:3 * P], k_tok[:, c, :], vdec[d][:, :], start=True, stop=True).then_inc(kv_mm[d], 1)
            last.then_inc(o_mm, 1)
            gate_rows(h + GATE_HEADS, 15, 16, 4)
            pe.wait_ge(o_sq, h + 1)
            pe.matmul(bank[0][:, :], ones[:, :], nsq[0][:, :], start=True, stop=True).then_inc(o_summed, 1)

        pe.wait_ge(o_rinv, HEADS)
        pe.wait_ge(gate_out, 2 * BLOCKS + 1)
        with pe.Fori(0, BLOCKS // 2) as i:
            for b in range(2):
                pe.wait_ge(merged[b], i + 1)

                def ready(k):
                    if b == 0:
                        pe.wait_ge(re_lo, ROWS * j + k + 1)

                for j in range(2):
                    slot(i * 4 + (S_MERGE + 2 * b + j), j, bank[4 * b + 2 * j:4 * b + 2 * j + 2], y_hi, y_lo, ROWS * (1 - j), True, True, ready)

        def out_block(i, b):
            pe.wait_ge(x1_done, i * 2 + (b + 1))

            def ready(k):
                if b == 0 and k % 2 == 0:
                    pe.wait_ge(m_lo, (ROWS * j + k) // 2 + 1)

            for j in range(2):
                slot(i * 4 + (S_OUT + 2 * b + j), j, bank[2 * b:2 * b + 2], act_hi, act_lo, ROWS * j, j == 0, j == 1, ready)

        for b in range(2):
            pe.wait_ge(merged[b], BLOCKS // 2 + 1)
            out_block(0, b)
        sum_squares(KT // 2, 0, start=True)
        with pe.Fori(1, OUT_BODIES) as i:
            for b in range(2):
                out_block(i, b)
                sum_squares(i * 2 + (KT // 2 - 1 + b), 1 - b)
        sum_squares(KT - 1, 1, stop=True)

        pe.wait_ge(x1_done, 2 * OUT_BODIES + 2)
        with pe.Fori(0, CHUNKS) as c:
            with pe.Fori(0, 2) as i:
                for b in range(2):
                    pe.wait_ge(u_relu[b], c * 2 + i + 1)
                    pe.wait_ge(y_added[b], c * 2 + 1)
                    for j in range(2):

                        def ready(k):
                            if b == 0:
                                pe.wait_ge(h_lo, KT + ROWS * j + k + 1)

                        slot(c * 16 + i * 4 + (S_MLP + 2 * b + j), j, bank[2 * b:2 * b + 2], act_hi, act_lo, ROWS * j, j == 0, j == 1, ready)
            with pe.Fori(0, 2) as i:
                for j in range(4):
                    pe.wait_ge(y_added[j], c * 2 + i + 1)
                    if j < 2:
                        pe.wait_ge(u_relu[j], c * 2 + 3)

                    def ready(k):
                        if j == 0 and k % 2 == 0:
                            pe.wait_ge(u_ready[(k // 2) % 2], c * 2 + (k // 4 + 2))

                    slot(c * 16 + i * 4 + (S_MLP + 8 + j), j % 2, bank[2 * j:2 * j + 2], u_hi, u_lo, 0, True, True, ready)

    ctx.close()


def _slots(w, k0, c0):
    part = w[k0:k0 + ROWS * P, c0:c0 + COLS]
    return part.reshape(ROWS, P, COLS).transpose(1, 0, 2).reshape(P, SLOT)


def _column(v):
    return np.asarray(v).reshape(-1, P).T


def _stream(w_in, w_dn, w_sw, w_out, w_mi, w_mo):
    small = 2 * D + 0
    out = np.empty((N_SLOTS, P, SLOT), np.float32)
    at = [0]

    def put(w, k0, c0):
        out[at[0]] = _slots(w, k0, c0)
        at[0] += 1

    def columns(w, c0, c1):
        for c in range(c0, c1, COLS):
            for k in range(0, w.shape[0], ROWS * P):
                put(w, k, c)

    sw = small + 4 * HEADS
    gates = sw + (HEADS + 2 * KV_HEADS) * P
    columns(w_in, sw, gates)
    columns(w_in, 0, small)
    columns(w_in, gates, gates + 2 * D)
    for j in range(BLOCKS):
        columns(w_sw, j * COLS, (j + 1) * COLS)
        columns(w_dn, j * COLS, (j + 1) * COLS)
    columns(w_out, 0, D)
    for c in range(CHUNKS):
        columns(w_mi, c * ROWS * P, (c + 1) * ROWS * P)
        columns(w_mo[c * ROWS * P:(c + 1) * ROWS * P], 0, D)
    assert at[0] == N_SLOTS
    return out


def kernel(x, c, w_ada, b_ada, norm1_w, w_in, conv_w, dn_a_log, dn_dt_bias, dn_out_norm_w,
           w_dn_proj, q_norm_w, k_norm_w, sink, w_swa_proj, w_out, norm2_w, w_mlp_in, w_mlp_out):
    import concourse.bacc as bacc
    from concourse.bass_utils import run_bass_kernel_spmd

    def row(v, n):
        return np.broadcast_to(np.asarray(v, np.float32).reshape(1, n), (P, n))

    w_in = np.asarray(w_in)[0]
    params = np.concatenate([
        _column(c), _column(b_ada), _column(norm1_w), _column(norm2_w),
        np.asarray(conv_w)[0].reshape(CONV_K, QKV_T, P).transpose(2, 1, 0).reshape(P, QKV_T * CONV_K),
        _column(dn_out_norm_w), _column(q_norm_w), _column(k_norm_w),
        row(dn_dt_bias, 16), row(dn_a_log, 16), row(sink, HEADS),
        row([EPS, math.log(SCALE), 1.0], 3)], axis=1)
    arrays = {
        "wstream": _stream(w_in, *(np.asarray(w)[0] for w in (w_dn_proj, w_swa_proj, w_out, w_mlp_in, w_mlp_out))),
        "adastream": np.asarray(w_ada)[0].reshape(4, 4, P, ADA_G, 512).transpose(3, 0, 2, 1, 4).reshape(4 * ADA_G, P, SLOT),
        "wsmall": w_in[:, 2 * D:2 * D + 32].reshape(KT, P, 32).transpose(1, 0, 2).reshape(P, KT * 32),
        "xT": np.asarray(x)[0].T,
        "params": params,
        "maskc": masks(),
    }
    arrays = {f"in_{n}_dram": np.ascontiguousarray(a) for n, a in arrays.items()}
    nc = bacc.Bacc("TRN2", target_bir_lowering=False, num_devices=1)
    args = [nc.dram_tensor(n, a.shape, mybir.dt.from_np(a.dtype), kind="ExternalInput").ap() for n, a in arrays.items()]
    args.append(nc.dram_tensor("out_0_dram", (D, SEQ), FP32, kind="ExternalOutput").ap())
    hybrid_block_kernel(nc, *args)
    r = run_bass_kernel_spmd(nc, [arrays], core_ids=[0])
    return np.ascontiguousarray(r.results[0]["out_0_dram"].T)[None]
```
